# Optimizing a Trainium2 kernel written in Bass

```python
import functools
import jax, jax.numpy as jnp
from jax import lax
import numpy as np

D_MODEL = 1024
BATCH = 1
SEQ = 256
DEPTH = 1
DEC_BATCH = 8
DEC_SEQ = 8
PAST_LEN = 256
PAGE_SIZE = 128

N_HEADS = 16
HEAD_DIM = D_MODEL // N_HEADS
D_ATTN = N_HEADS * HEAD_DIM
D_RNN = D_MODEL
N_RNN_BLOCKS = 16
RNN_BLOCK = D_RNN // N_RNN_BLOCKS
CONV_W = 4
LRU_C = 8.0
N_EXPERTS = 32
TOP_K = 4
D_EXPERT = D_MODEL
SWIGLU_LIMIT = 7.0
SWIGLU_ALPHA = 1.702
Q_BLOCK = 128
ROW_BLOCK = 128
EPS = 1e-6
D_IN = D_RNN + 3 * D_ATTN + N_HEADS + 2 * D_MODEL

kernel_name = "hybrid_rglru_fox_moe_step"

def rms_norm(x, g):
    xf = x.astype(jnp.float32)
    y = xf * lax.rsqrt(jnp.mean(xf * xf, axis=-1, keepdims=True) + EPS)
    return (y * g.astype(jnp.float32)).astype(x.dtype)

def causal_conv(x, prev, w, b):
    s = x.shape[1]
    xp = jnp.concatenate([prev.astype(x.dtype), x], axis=1)
    y = b
    for j in range(CONV_W):
        y = y + w[j] * xp[:, j:j + s]
    return y, xp[:, -(CONV_W - 1):]

def block_diag_linear(x, w, b):
    bsz, s, _ = x.shape
    xb = x.reshape(bsz, s, N_RNN_BLOCKS, RNN_BLOCK)
    return jnp.einsum('bsnc,ncd->bsnd', xb, w).reshape(bsz, s, D_RNN) + b

def rg_lru(x, h0, lam, w_a, b_a, w_x, b_x, reset_first):
    r = jax.nn.sigmoid(block_diag_linear(x, w_a, b_a).astype(jnp.float32))
    i = jax.nn.sigmoid(block_diag_linear(x, w_x, b_x).astype(jnp.float32))
    log_a = -LRU_C * r * jax.nn.softplus(-lam.astype(jnp.float32))
    a = jnp.exp(log_a)
    mult = jnp.sqrt(-jnp.expm1(2.0 * log_a))
    if reset_first:
        mult = mult.at[:, 0].set(1.0)
    u = mult * i * x.astype(jnp.float32)
    u = u.at[:, 0].add(a[:, 0] * h0.astype(jnp.float32))

    def combine(left, right):
        a_l, b_l = left
        a_r, b_r = right
        return a_l * a_r, a_r * b_l + b_r

    _, h = lax.associative_scan(combine, (a, u), axis=1)
    return h.astype(x.dtype), h[:, -1]

def fox_prompt(q, k, v, logf):
    s_len = q.shape[1]
    scale = HEAD_DIM ** -0.5
    ft = jnp.swapaxes(jnp.cumsum(logf, axis=1), 1, 2)
    outs = []
    for blk in range(s_len // Q_BLOCK):
        q0 = blk * Q_BLOCK
        kend = q0 + Q_BLOCK
        sc = jnp.einsum('bqhd,bkhd->bhqk', q[:, q0:kend], k[:, :kend]).astype(jnp.float32) * scale
        bias = ft[:, :, q0:kend, None] - ft[:, :, None, :kend]
        mask = jnp.arange(kend)[None, :] <= (q0 + jnp.arange(Q_BLOCK))[:, None]
        p = jax.nn.softmax(jnp.where(mask, sc + bias, -jnp.inf), axis=-1)
        outs.append(jnp.einsum('bhqk,bkhd->bqhd', p.astype(v.dtype), v[:, :kend]))
    return jnp.concatenate(outs, axis=1)

def fox_sample(q, k, v, logf, cache_k, cache_v, cache_logf, page_table):
    db, ds = q.shape[:2]
    past = page_table.shape[1] * PAGE_SIZE
    scale = HEAD_DIM ** -0.5
    k_all = jnp.concatenate([cache_k[page_table].reshape(db, past, N_HEADS, HEAD_DIM).astype(k.dtype), k], axis=1)
    v_all = jnp.concatenate([cache_v[page_table].reshape(db, past, N_HEADS, HEAD_DIM).astype(v.dtype), v], axis=1)
    lf_all = jnp.concatenate([cache_logf[page_table].reshape(db, past, N_HEADS).astype(jnp.float32), logf], axis=1)
    ft = jnp.swapaxes(jnp.cumsum(lf_all, axis=1), 1, 2)
    sc = jnp.einsum('bqhd,bkhd->bhqk', q, k_all).astype(jnp.float32) * scale
    bias = ft[:, :, past:, None] - ft[:, :, None, :]
    mask = jnp.arange(past + ds)[None, :] <= (past + jnp.arange(ds))[:, None]
    p = jax.nn.softmax(jnp.where(mask, sc + bias, -jnp.inf), axis=-1)
    return jnp.einsum('bhqk,bkhd->bqhd', p.astype(v_all.dtype), v_all)

def mixer(h, prev_conv, h0, reset_first, attn_fn, lw):
    bsz, s, _ = h.shape
    z = h @ lw['w_in']
    cuts = [D_RNN, D_RNN + D_ATTN, D_RNN + 2 * D_ATTN, D_RNN + 3 * D_ATTN,
            D_RNN + 3 * D_ATTN + N_HEADS, D_RNN + 3 * D_ATTN + N_HEADS + D_MODEL]
    x_rnn, q, k, v, f_logit, g_a, g_b = jnp.split(z, cuts, axis=-1)
    xc, conv_state = causal_conv(x_rnn, prev_conv, lw['conv_w'], lw['conv_b'])
    y_rnn, h_last = rg_lru(xc, h0, lw['rg_lambda'], lw['rg_w_a'], lw['rg_b_a'], lw['rg_w_x'], lw['rg_b_x'], reset_first)
    q = q.reshape(bsz, s, N_HEADS, HEAD_DIM)
    k = k.reshape(bsz, s, N_HEADS, HEAD_DIM)
    v = v.reshape(bsz, s, N_HEADS, HEAD_DIM)
    logf = jax.nn.log_sigmoid((f_logit + lw['b_forget']).astype(jnp.float32))
    y_attn = attn_fn(q, k, v, logf).reshape(bsz, s, D_ATTN)
    merged = jax.nn.sigmoid(g_a) * y_rnn + jax.nn.sigmoid(g_b) * y_attn
    return merged @ lw['w_out'], (k, v, logf, conv_state, h_last)

def moe(h, w_router, b_router, w_gate_up, b_gate_up, w_down, b_down):
    bsz, s, d = h.shape
    t = h.reshape(-1, d)
    n_tok = t.shape[0]
    logits = (t @ w_router + b_router).astype(jnp.float32)
    top_v, top_e = lax.top_k(logits, TOP_K)
    gate = jax.nn.softmax(top_v, axis=-1)
    n_assign = n_tok * TOP_K
    flat_e = top_e.reshape(-1)
    flat_tok = jnp.repeat(jnp.arange(n_tok, dtype=jnp.int32), TOP_K)
    flat_w = gate.reshape(-1)
    order = jnp.argsort(flat_e)
    se, stok, sw = flat_e[order], flat_tok[order], flat_w[order]
    counts = jnp.zeros((N_EXPERTS,), jnp.int32).at[flat_e].add(1)
    padded = (counts + ROW_BLOCK - 1) // ROW_BLOCK * ROW_BLOCK
    start = jnp.cumsum(counts) - counts
    pend = jnp.cumsum(padded)
    pstart = pend - padded
    dest = pstart[se] + jnp.arange(n_assign, dtype=jnp.int32) - start[se]
    n_blocks = -(-n_assign // ROW_BLOCK) + N_EXPERTS
    n_rows = n_blocks * ROW_BLOCK
    row_tok = jnp.zeros((n_rows,), jnp.int32).at[dest].set(stok)
    row_w = jnp.zeros((n_rows,), jnp.float32).at[dest].set(sw)
    block_e = jnp.minimum(jnp.searchsorted(pend, jnp.arange(n_blocks, dtype=jnp.int32) * ROW_BLOCK, side='right'), N_EXPERTS - 1)
    xr = t[row_tok].reshape(n_blocks, ROW_BLOCK, d)

    def expert_block(args):
        xb, e = args
        gu = xb @ w_gate_up[e] + b_gate_up[e]
        x_glu = jnp.minimum(gu[:, :D_EXPERT], SWIGLU_LIMIT)
        x_lin = jnp.clip(gu[:, D_EXPERT:], -SWIGLU_LIMIT, SWIGLU_LIMIT)
        act = x_glu * jax.nn.sigmoid(SWIGLU_ALPHA * x_glu) * (x_lin + 1.0)
        return act @ w_down[e] + b_down[e]

    yr = lax.map(expert_block, (xr, block_e)).reshape(n_rows, d)
    y = jax.ops.segment_sum(yr * row_w[:, None].astype(yr.dtype), row_tok, num_segments=n_tok)
    return y.reshape(bsz, s, d)

def trunk_layer(x, c, lw, prev_conv, h0, reset_first, attn_fn):
    ada = jax.nn.silu(c) @ lw['w_ada'] + lw['b_ada']
    sh1, sc1, gt1, sh2, sc2, gt2 = [a[:, None, :] for a in jnp.split(ada, 6, axis=-1)]
    h = rms_norm(x, lw['g_mix_pre']) * (1.0 + sc1) + sh1
    out, st = mixer(h, prev_conv, h0, reset_first, attn_fn, lw)
    x = x + gt1 * rms_norm(out, lw['g_mix_post'])
    h = rms_norm(x, lw['g_ffn_pre']) * (1.0 + sc2) + sh2
    f = moe(h, lw['w_router'], lw['b_router'], lw['w_gate_up'], lw['b_gate_up'], lw['w_down'], lw['b_down'])
    x = x + gt2 * rms_norm(f, lw['g_ffn_post'])
    return x, st

def setup_inputs(seed: int = 0) -> dict:
    key = jax.random.key(seed)
    ks = iter(jax.random.split(key, 40))

    def nrm(shape, scale):
        return scale * jax.random.normal(next(ks), shape, jnp.float32)

    n_pages = PAST_LEN // PAGE_SIZE
    n_pool = (DEC_BATCH * n_pages * 5 + 3) // 4
    perm = jax.random.permutation(next(ks), n_pool)
    page_table = perm[:DEC_BATCH * n_pages].reshape(DEC_BATCH, n_pages).astype(jnp.int32)
    a0 = jax.random.uniform(next(ks), (DEPTH, D_RNN), jnp.float32, 0.9, 0.999)
    p = a0 ** (1.0 / LRU_C)
    rg_lambda = jnp.log(p) - jnp.log1p(-p)
    b_forget = jax.random.uniform(next(ks), (DEPTH, N_HEADS), jnp.float32, 1.0, 4.0)
    cache_logf = jax.nn.log_sigmoid(3.0 + nrm((DEPTH, n_pool, PAGE_SIZE, N_HEADS), 1.0))
    dm = D_MODEL ** -0.5
    return {
        'x_prompt': nrm((BATCH, SEQ, D_MODEL), 1.0),
        'x_sample': nrm((DEC_BATCH, DEC_SEQ, D_MODEL), 1.0),
        'cache_k': nrm((DEPTH, n_pool, PAGE_SIZE, N_HEADS, HEAD_DIM), 1.0),
        'cache_v': nrm((DEPTH, n_pool, PAGE_SIZE, N_HEADS, HEAD_DIM), 1.0),
        'cache_logf': cache_logf,
        'state_conv': nrm((DEPTH, DEC_BATCH, CONV_W - 1, D_RNN), 1.0),
        'state_h': nrm((DEPTH, DEC_BATCH, D_RNN), 0.5),
        'page_table': page_table,
        'c_prompt': nrm((BATCH, D_MODEL), 1.0),
        'c_sample': nrm((DEC_BATCH, D_MODEL), 1.0),
        'w_ada': nrm((DEPTH, D_MODEL, 6 * D_MODEL), 0.3 * dm),
        'b_ada': nrm((DEPTH, 6 * D_MODEL), 0.1),
        'g_mix_pre': 1.0 + nrm((DEPTH, D_MODEL), 0.05),
        'g_mix_post': 1.0 + nrm((DEPTH, D_MODEL), 0.05),
        'w_in': nrm((DEPTH, D_MODEL, D_IN), dm),
        'b_forget': b_forget,
        'conv_w': nrm((DEPTH, CONV_W, D_RNN), CONV_W ** -0.5),
        'conv_b': nrm((DEPTH, D_RNN), 0.02),
        'rg_w_a': nrm((DEPTH, N_RNN_BLOCKS, RNN_BLOCK, RNN_BLOCK), RNN_BLOCK ** -0.5),
        'rg_b_a': nrm((DEPTH, D_RNN), 0.02),
        'rg_w_x': nrm((DEPTH, N_RNN_BLOCKS, RNN_BLOCK, RNN_BLOCK), RNN_BLOCK ** -0.5),
        'rg_b_x': nrm((DEPTH, D_RNN), 0.02),
        'rg_lambda': rg_lambda,
        'w_out': nrm((DEPTH, D_MODEL, D_MODEL), dm),
        'g_ffn_pre': 1.0 + nrm((DEPTH, D_MODEL), 0.05),
        'g_ffn_post': 1.0 + nrm((DEPTH, D_MODEL), 0.05),
        'w_router': nrm((DEPTH, D_MODEL, N_EXPERTS), dm),
        'b_router': nrm((DEPTH, N_EXPERTS), 0.01),
        'w_gate_up': nrm((DEPTH, N_EXPERTS, D_MODEL, 2 * D_EXPERT), dm),
        'b_gate_up': nrm((DEPTH, N_EXPERTS, 2 * D_EXPERT), 0.01),
        'w_down': nrm((DEPTH, N_EXPERTS, D_EXPERT, D_MODEL), D_EXPERT ** -0.5),
        'b_down': nrm((DEPTH, N_EXPERTS, D_MODEL), 0.01),
    }

def reference(x_prompt, x_sample, cache_k, cache_v, cache_logf, state_conv, state_h, page_table,
              c_prompt, c_sample, w_ada, b_ada, g_mix_pre, g_mix_post, w_in, b_forget,
              conv_w, conv_b, rg_w_a, rg_b_a, rg_w_x, rg_b_x, rg_lambda, w_out,
              g_ffn_pre, g_ffn_post, w_router, b_router, w_gate_up, b_gate_up, w_down, b_down):
    yp, ys = x_prompt, x_sample
    kp_l, vp_l, lfp_l, cvp_l, hp_l = [], [], [], [], []
    ks_l, vs_l, lfs_l, cvs_l, hs_l = [], [], [], [], []
    for l in range(DEPTH):
        lw = {
            'w_ada': w_ada[l], 'b_ada': b_ada[l], 'g_mix_pre': g_mix_pre[l], 'g_mix_post': g_mix_post[l],
            'w_in': w_in[l], 'b_forget': b_forget[l], 'conv_w': conv_w[l], 'conv_b': conv_b[l],
            'rg_w_a': rg_w_a[l], 'rg_b_a': rg_b_a[l], 'rg_w_x': rg_w_x[l], 'rg_b_x': rg_b_x[l],
            'rg_lambda': rg_lambda[l], 'w_out': w_out[l], 'g_ffn_pre': g_ffn_pre[l], 'g_ffn_post': g_ffn_post[l],
            'w_router': w_router[l], 'b_router': b_router[l], 'w_gate_up': w_gate_up[l],
            'b_gate_up': b_gate_up[l], 'w_down': w_down[l], 'b_down': b_down[l],
        }
        zero_conv = jnp.zeros((yp.shape[0], CONV_W - 1, D_RNN), yp.dtype)
        zero_h = jnp.zeros((yp.shape[0], D_RNN), jnp.float32)
        yp, (kp, vp, lfp, cvp, hp) = trunk_layer(yp, c_prompt, lw, zero_conv, zero_h, True, fox_prompt)
        attn_sample = functools.partial(fox_sample, cache_k=cache_k[l], cache_v=cache_v[l],
                                        cache_logf=cache_logf[l], page_table=page_table)
        ys, (ks, vs, lfs, cvs, hs) = trunk_layer(ys, c_sample, lw, state_conv[l], state_h[l], False, attn_sample)
        kp_l.append(kp); vp_l.append(vp); lfp_l.append(lfp); cvp_l.append(cvp); hp_l.append(hp)
        ks_l.append(ks); vs_l.append(vs); lfs_l.append(lfs); cvs_l.append(cvs); hs_l.append(hs)
    return (yp, ys,
            jnp.stack(kp_l), jnp.stack(vp_l), jnp.stack(lfp_l), jnp.stack(cvp_l), jnp.stack(hp_l),
            jnp.stack(ks_l), jnp.stack(vs_l), jnp.stack(lfs_l), jnp.stack(cvs_l), jnp.stack(hs_l))


_drawn_inputs = setup_inputs


def setup_inputs(seed=0):
    import zlib

    import numpy as np

    out = dict(_drawn_inputs(seed))
    spreads = {}
    factors = {'rg_b_a': 8.0,
     'rg_b_x': 6.814,
     'g_ffn_post': 5.44,
     'b_router': 3.109,
     'b_gate_up': 8.0,
     'b_down': 8.0}
    for name, (base, spread) in spreads.items():
        noise = np.random.default_rng([zlib.crc32(name.encode()), seed]).standard_normal(out[name].shape)
        drawn = base * np.exp(spread * noise) if base else spread * noise
        out[name] = __import__('jax').numpy.asarray(drawn.astype(out[name].dtype))
    for name, factor in factors.items():
        out[name] = (out[name] * factor).astype(out[name].dtype)
    return out
```

```python
from contextlib import ExitStack

import concourse.bass as bass
from concourse import mybir

CAP = 64


class Chain:

    def __init__(self, eng, sem, base=None):
        self.eng, self.sem, self.base, self.n = eng, sem, base, 0

    def later(self, ins):
        ins.then_inc(self.sem, 1)
        self.n += 1

    def __call__(self, ins):
        self.later(ins)
        self.eng.wait_ge(self.sem, self.n if self.base is None else self.base + self.n)


def hybrid_layer(nc, x_prompt, x_sample, cache_k, cache_v, cache_logf, state_conv, state_h, page_table,
                 c_prompt, c_sample, w_ada, b_ada, g_mix_pre, g_mix_post, w_in, b_forget,
                 conv_w, conv_b, rg_w_a, rg_b_a, rg_w_x, rg_b_x, rg_lambda, w_out,
                 g_ffn_pre, g_ffn_post, w_router, b_router, w_gate_up, b_gate_up, w_down, b_down,
                 y_prompt, y_sample, k_prompt, v_prompt, logf_prompt, conv_prompt, h_prompt,
                 k_sample, v_sample, logf_sample, conv_sample, h_sample):
    f32, i32, u32 = mybir.dt.float32, mybir.dt.int32, mybir.dt.uint32
    ALU, ACT, AX = mybir.AluOpType, mybir.ActivationFunctionType, mybir.AxisListType
    ds = bass.ds

    D = x_prompt.shape[2]
    NT = D // 128
    SP_, DB, DS = x_prompt.shape[1], x_sample.shape[0], x_sample.shape[1]
    NS = DB * DS
    T = SP_ + NS
    TT = 3
    TROWS = [128, 128, NS]
    NR = 1 + DB
    H, HD = cache_k.shape[3], cache_k.shape[4]
    PG, NPOOL, NPG = cache_k.shape[2], cache_k.shape[1], page_table.shape[1]
    PAST = PG * NPG
    E, TOPK = w_router.shape[2], 4
    CW = conv_w.shape[1]
    SEG = CW - 1 + DS
    XW = CW - 1 + SP_ + DB * SEG
    OW = XW - (CW - 1)
    S0 = SP_ + CW - 1
    FW = SP_ + DB * (PAST + DS)
    EPS, LIMIT, ALPHA, SCALE, LRU_C = 1e-6, 7.0, 1.702, float(HD) ** -0.5, 8.0
    NEG = -1e30
    PAIRS, ROUNDS, SL = E // 2, -(-T // CAP), 2 * CAP
    RCOLS = E * (ROUNDS + 1)

    ctx = ExitStack()
    with ctx:
        def sb(name, shape, dt=f32):
            return ctx.enter_context(nc.sbuf_tensor(name, shape, dt))

        def sem(name):
            return ctx.enter_context(nc.semaphore(name))

        wgu = sb("wgu", [128, 4, 2, 2 * D])
        wdn = sb("wdn", [128, 2, 4, D])
        xT = sb("xT", [128, NT, T])
        hT = sb("hT", [128, NT, T])
        qT = sb("qT", [128, NT, T])
        kT = sb("kT", [128, NT, T])
        gaT = sb("gaT", [128, NT, T])
        gbT = sb("gbT", [128, NT, T])
        tok = sb("tok", [128, TT, D])
        work = sb("work", [128, 8280])
        ident = sb("ident", [128, 128])
        ones = sb("ones", [128, 128])
        ada = sb("ada", [128, 6 * NT, NR])
        Gm = sb("Gm", [128, 4, NT, NR])
        vecT = sb("vecT", [128, 472])
        wr = sb("wr", [128, NT, E])
        tiny = sb("tiny", [128, 136])

        wstage = [wgu[:, s, :, :].rearrange("p a n -> p (a n)").rearrange("p (k n) -> p k n", k=NT) for s in range(3)]
        fr = wgu[:, 3, :, :].rearrange("p a n -> p (a n)")
        Ssb = fr[:, 0:1152].rearrange("p (s n) -> p s n", s=3)
        PTs = fr[:, 1152:1920].rearrange("p (s n) -> p s n", s=2)
        mask = fr[:, 1920:2304]
        smask = fr[:, 2304:2304 + 2 * NS - DS]
        lfc = fr[:, 2432:2688].rearrange("p (g h) -> p g h", h=H)
        wf = fr[:, 2688:2816].rearrange("p (k h) -> p k h", h=H)
        onesf = fr[:, 2816:2816 + PAST + DS]
        st36 = fr[:, 3080:3080 + NT * 36].rearrange("p (t c) -> p t c", c=36)
        rs = fr[:, 3368:3688]
        lfz = fr[0:H, 3688:4008]
        lftok = fr[:, 4008:4056].rearrange("p (t h) -> p t h", h=H)
        rg = wdn[:, :, :, :].rearrange("p a k n -> p (a k n)")
        xc = rg[:, 0:NT * OW].rearrange("p (t c) -> p t c", t=NT)
        R = rg[:, NT * OW:2 * NT * OW].rearrange("p (t c) -> p t c", t=NT)
        wax = rg[:, 2 * NT * OW:2 * NT * OW + 2048].rearrange("p (g t c) -> p g t c", g=2, t=NT)
        kv = rg.rearrange("p (s g n) -> p s g n", s=2, g=4)

        NX, NO = NT * XW, NT * OW
        xp = work[:, 0:NX].rearrange("p (t c) -> p t c", t=NT)
        Dn = work[:, 0:NO].rearrange("p (t c) -> p t c", t=NT)
        Af = work[:, NX:NX + NO]
        Uf = work[:, NX + NO:NX + 2 * NO]
        A = Af.rearrange("p (t c) -> p t c", t=NT)
        U = Uf.rearrange("p (t c) -> p t c", t=NT)
        ktok = work[:, NX:NX + TT * D].rearrange("p (t n) -> p t n", t=TT)
        vrows = work[:, 5900:6540].rearrange("p (g n) -> p g n", g=5)
        strow = fr[0:36, 0:D]
        KT = work[:, 0:4096].rearrange("p (s t c) -> p s t c", s=2, t=NT)
        Qbd = work[:, 4096:6144].rearrange("p (s t c) -> p s t c", s=2, t=NT)
        Ss = work[:, 6144:6784].rearrange("p (s c) -> p s c", s=2)
        PT2 = work[:, 6784:7552].rearrange("p (s c) -> p s c", s=2)
        at = [0]

        def carve(n, area=work, limit=8280):
            at[0] += n
            assert at[0] <= limit
            return area[:, at[0] - n:at[0]]

        XT = carve(NT * SL).rearrange("p (t s) -> p t s", t=NT)
        glu = carve(NT * CAP).rearrange("p (t s) -> p t s", t=NT)
        lin = carve(NT * CAP).rearrange("p (t s) -> p t s", t=NT)
        sig = carve(NT * CAP).rearrange("p (t s) -> p t s", t=NT)
        act = carve(NT * CAP).rearrange("p (t s) -> p t s", t=NT)
        YT = carve(NT * SL).rearrange("p (t s) -> p t s", t=NT)
        Ysb = carve(D)[0:SL, :]
        sel = carve(TT * SL).rearrange("p (t s) -> p t s", t=TT)
        selw = carve(TT * SL).rearrange("p (t s) -> p t s", t=TT)
        Cnext = carve(T)[0:SL, :]
        Ccur = carve(T)[0:SL, :]
        bgu = carve(2 * NT * E)
        tri = carve(128)
        slot = carve(CAP)
        yrow = work[:, 0:TT * D].rearrange("p (t n) -> p t n", t=TT)
        qf = qT[:, :, :].rearrange("p t n -> p (t n)")
        kf = kT[:, :, :].rearrange("p t n -> p (t n)")
        gaf = gaT[:, :, :].rearrange("p t n -> p (t n)")
        rank = qf[:, 0:TT * RCOLS].rearrange("p (t c) -> p t c", t=TT)
        gate = qf[:, TT * RCOLS:2 * TT * RCOLS].rearrange("p (t c) -> p t c", t=TT)
        lg = kf[:, 0:96].rearrange("p (t e) -> p t e", t=TT)
        top = kf[:, 96:120].rearrange("p (t e) -> p t e", t=TT)
        topi = kf[:, 120:144].bitcast(u32).rearrange("p (t e) -> p t e", t=TT)
        topf = kf[:, 144:168].rearrange("p (t e) -> p t e", t=TT)
        tope = kf[:, 168:192].rearrange("p (t e) -> p t e", t=TT)
        toks = kf[:, 192:216].rearrange("p (t e) -> p t e", t=TT)
        hit = kf[:, 216:312].rearrange("p (t e) -> p t e", t=TT)
        chosen = kf[:, 312:408].rearrange("p (t e) -> p t e", t=TT)
        wtok = kf[:, 408:504].rearrange("p (t e) -> p t e", t=TT)
        rk0 = kf[:, 504:600].rearrange("p (t e) -> p t e", t=TT)
        exi = kf[:, 600:600 + E]
        WT = kf[0:E, 640:640 + T]
        bdn = gaf[0:E, 0:D]
        burows = gaf[:, D:D + 512].rearrange("p (g n) -> p g n", g=4)
        rs2 = gaf[:, 1600:1600 + T]
        F = hT[0:H, :, :].rearrange("p t n -> p (t n)")[:, 0:FW]

        def few(a, n, parts=128):
            return tiny[0:parts, a:a + n]

        sp8, t8, s8, a8 = few(0, 8), few(8, 8), few(16, 8), few(24, 8)
        bfg = few(32, 1, H)
        brow = few(33, E, 1)
        nm = few(66, 6).rearrange("p (s n) -> p s n", s=3)
        rsum = few(72, 6).rearrange("p (s n) -> p s n", s=3)
        sst = few(78, 6).rearrange("p (s n) -> p s n", s=2)
        cmax, rounds_f, over = few(84, 1), few(85, 1), few(86, 5)
        rounds_i = few(92, 1).bitcast(i32)
        steps_i = few(94, 5).bitcast(i32)
        steps = few(100, 5)
        ptab = few(106, 16, 1).bitcast(i32)
        sigc = kf[:, 0:NR * NT]
        smask8 = kf[0:DS, 1200:1200 + 2 * NS - DS]
        qsel = kf[0:DS, 1400:1400 + H * DS]
        sioti = kf[:, 1000:1064].bitcast(i32)
        eioti = kf[:, 1064:1064 + E].bitcast(i32)

        B = [ctx.enter_context(nc.psum_tensor(f"bank{i}", [128, 512], f32)) for i in range(8)]

        V = dict(g_mix_pre=0, g_mix_post=8, g_ffn_pre=16, g_ffn_post=24, conv_b=32, rg_b_a=40, rg_b_x=48,
                 rg_lambda=56, conv_w=64, b_ada=96, c=144, h0=216, conv=280)

        hsel = vecT[0:H, 280:280 + H * DS]

        def vec(name, n=NT):
            return vecT[:, V[name]:V[name] + n]

        names = """smask8_made qsel_made hsel_made smask_made consts_made ident_made x_in rows_in small_in pages_in cachef_in rgw_zeroed rgw_in
            rows_ps vec_made spn_made csig_made c_made xT_ps xT_made xT_sq sum_ps ms_made rs_made ada_ps ada_made h_made
            chunk_free job_ps job_ev tr_ps tr_ev xp_edges conv_made absw_made expw_made lf_made decay_in decay_out
            den_made mult_made st_made rg_done F_made
            scores_ps scores_read negmax_made exp_done probs_made PT_ps PT_ev py_ps py_read
            qbd_zero qbd_made KT_ps KT_ev sscores_ps sscores_read snegmax_made sexp_done sprobs_made
            sPT_ps sPT_ev sy_ps sy_read merged
            out_ps out_read out_sq rs_sq_ps x1_made x1_sq h2_made h2_ps h2tok_made
            late_in bgu_ps bgu_made slot_made router_ps logits_made topmax_made topexp_made chosen_made rank_ps wt_ps wt_made
            fT_ps fT_made tables_made rounds_made
            gu_free dn_free gu_done glu_made act_made sig_made gu_read dn_done YT_made sel_made gather_ps XT_made
            cT_ps cT_read C_made C_moved yt_ps Y_made scatter_ps scatter_read
            f_sq f_sum y_ready y_ps y_made chain_dve chain_act chain_pool chain_moe
            out_kv out_states out_y""".split()
        s = {n: sem(n) for n in names}
        chunk_in = [sem(f"chunk_in{i}") for i in range(3)]
        k_in = [sem(f"k_in{i}") for i in range(2)]
        v_in = [sem(f"v_in{i}") for i in range(2)]
        gu_in = [sem(f"gu_in{i}") for i in range(4)]
        dn_in = [sem(f"dn_in{i}") for i in range(2)]

        adav = w_ada[0].rearrange("(k p) n -> p k n", p=128)
        winv = w_in[0].rearrange("(k p) n -> p k n", p=128)
        woutv = w_out[0].rearrange("(k p) n -> p k n", p=128)
        FCOL = 4 * D
        ZCOL = dict(x=0, q=D, k=2 * D, v=3 * D, ga=FCOL + H, gb=FCOL + H + D)
        ZORD = ["v", "k", "x", "q", "ga", "gb"]
        CHUNKS = [adav[:, :, 512 * i:512 * i + 512] for i in range(4)]
        CHUNKS += [winv[:, :, ZCOL[z] + 512 * i:ZCOL[z] + 512 * i + 512] for z in ZORD for i in range(2)]
        CHUNKS += [adav[:, :, 512 * i:512 * i + 512] for i in range(4, 12)]
        CHUNKS += [woutv[:, :, 512 * i:512 * i + 512] for i in range(2)]
        JOBS = [("v", t) for t in range(NT)] + [("k", t) for t in range(NT)] + [("x", t) for t in range(NT)]
        JOBS += [("f", 0)] + [("q", t) for t in range(NT)]
        JOBS += [("r", t) for t in range(NT)] + [("i", t) for t in range(NT)]
        JOBS += [("ga", t) for t in range(NT)] + [("gb", t) for t in range(NT)]
        LAST = {k: max(i for i, j in enumerate(JOBS) if j[0] == k) + 1 for k in "v k x f q r i ga gb".split()}
        G_V, G_K, G_LF, G_CF, G_ST = 0, 6, 12, 13, 17
        block = ctx.enter_context(nc.Block())

        def page(eng, i):
            return eng.value_load(ptab[0:1, i:i + 1], min_val=0, max_val=NPOOL - 1)

        def moe_rounds(eng, pair):
            with eng.Fori(0, PAIRS) as i:
                pair(i, i)
            eng.wait_ge(s["rounds_made"], 1)
            n = eng.value_load(rounds_i[0:1, :], min_val=1, max_val=ROUNDS)
            with eng.Fori(1, ROUNDS) as r:
                with eng.If(r < n):
                    with eng.Fori(0, PAIRS) as i:
                        pair(r * PAIRS + i, i)
            return n * PAIRS

        @block.sync
        def _(eng):
            for name, src in (("x", (x_prompt[0].rearrange("(t p) n -> p t n", p=128), tok[:, 0:2, :])),
                              ("s", (x_sample.rearrange("b q n -> (b q) n"), tok[0:NS, 2, :]))):
                eng.dma_start(src[1], src[0]).then_inc(s["x_in"], 16)

            def tiles(v, o="(t p)"):
                return v.rearrange("o (t p) -> (o t) p", p=128)

            for at_, v in ((0, g_mix_pre), (8, g_mix_post), (16, g_ffn_pre), (24, g_ffn_post), (32, conv_b),
                           (40, rg_b_a), (48, rg_b_x), (56, rg_lambda), (64, conv_w[0])):
                rows = v.shape[0] * NT
                eng.dma_start(vrows[at_:at_ + rows, 0, :], tiles(v)).then_inc(s["rows_in"], 16)
            for at_, v in ((0, b_ada), (48, c_prompt), (56, c_sample)):
                rows = v.shape[0] * v.shape[1] // 128
                eng.dma_start(vrows[at_:at_ + rows, 1, :], tiles(v)).then_inc(s["rows_in"], 16)
            eng.dma_start(vrows[0:64, 2, :], tiles(state_h[0])).then_inc(s["rows_in"], 16)
            scv = state_conv[0].rearrange("b j (t p) -> (b j t) p", p=128)
            for i in range(2):
                eng.dma_start(vrows[0:96, 3 + i, :], scv[96 * i:96 * i + 96, :]).then_inc(s["rows_in"], 16)

            def chunk(c):
                if c >= 3:
                    eng.wait_ge(s["chunk_free"], c - 2)
                eng.dma_start(wstage[c % 3], CHUNKS[c]).then_inc(chunk_in[c % 3], 16)

            for c in range(3):
                chunk(c)
            eng.dma_start(ptab, page_table.rearrange("(o b) g -> o (b g)", o=1)).then_inc(s["pages_in"], 16)
            eng.dma_start(wf, winv[:, :, FCOL:FCOL + H]).then_inc(s["small_in"], 16)
            eng.dma_start(bfg, b_forget.rearrange("o h -> h o")).then_inc(s["small_in"], 16)
            eng.dma_start(wr[:, :, :], w_router[0].rearrange("(k p) e -> p k e", p=128)).then_inc(s["small_in"], 16)
            eng.dma_start(brow, b_router).then_inc(s["small_in"], 16)
            eng.wait_ge(s["rgw_zeroed"], 1)
            for g, w in enumerate((rg_w_a, rg_w_x)):
                wv = w[0].rearrange("(t two) c d -> two c t d", two=2)
                for two in range(2):
                    o = 64 * two
                    eng.dma_start(wax[o:o + 64, g, :, o:o + 64], wv[two]).then_inc(s["rgw_in"], 16)
            eng.wait_ge(s["pages_in"], 16)
            for i in range(DB * NPG):
                eng.dma_start(lfc[:, i, :], cache_logf[0, ds(page(eng, i), 1), :, :].rearrange("o p h -> (o p) h"))\
                    .then_inc(s["cachef_in"], 16)
            for c in range(3, len(CHUNKS)):
                chunk(c)
            eng.wait_ge(s["rg_done"], 1)
            for b in range(DB):
                for g, c, in_ in ((0, cache_k, k_in), (NPG, cache_v, v_in)):
                    if b >= 2 and g == 0:
                        eng.wait_ge(s["KT_ps"], 4 * (b - 1))
                    if b >= 2 and g:
                        eng.wait_ge(s["sy_ps"], b - 1)
                    for i in range(NPG):
                        eng.dma_start(kv[:, b % 2, g + i, :],
                                      c[0, ds(page(eng, NPG * b + i), 1), :, :, :].rearrange("o p h d -> (o p) (h d)"))\
                            .then_inc(in_[b % 2], 16)

            guv = w_gate_up[0].rearrange("e (c a p) n -> e c p a n", a=2, p=128)
            dnv = w_down[0].rearrange("e (c a p) n -> e c p a n", a=4, p=128)

            def pair(t, i):
                for half in range(2):
                    for c in range(4):
                        eng.wait_ge(s["gu_free"], 8 * t + (4 * half + c + 1))
                        eng.dma_start(wgu[:, c, :, :], guv[ds(2 * i + half, 1), c].rearrange("o p a n -> (o p) a n"))\
                            .then_inc(gu_in[c], 16)
                    for c in range(2):
                        eng.wait_ge(s["dn_free"], 4 * t + (2 * half + c + 1))
                        eng.dma_start(wdn[:, c, :, :], dnv[ds(2 * i + half, 1), c].rearrange("o p a n -> (o p) a n"))\
                            .then_inc(dn_in[c], 16)

            moe_rounds(eng, pair)

        @block.gpsimd
        def _(eng):
            link = Chain(eng, s["chain_pool"])
            link(eng.memset(ident[:, :], 0.0))
            eng.affine_select(out=ident[:, :], in_=ident[:, :], compare_op=ALU.not_equal, fill=1.0, base=0,
                              pattern=[[-1, 128]], channel_multiplier=1).then_inc(s["ident_made"], 1)
            eng.memset(ones[:, :], 1.0).then_inc(s["ident_made"], 1)
            eng.memset(wax, 0.0).then_inc(s["rgw_zeroed"], 1)
            link(eng.memset(mask, 0.0))
            for o in (0, 256):
                eng.affine_select(out=mask[:, o:o + 128], in_=mask[:, o:o + 128], compare_op=ALU.is_ge, fill=NEG,
                                  base=0, pattern=[[-1, 128]], channel_multiplier=1).then_inc(s["consts_made"], 1)
            J0 = NS - DS
            link(eng.memset(smask8, 0.0))
            link(eng.affine_select(out=smask8, in_=smask8, compare_op=ALU.is_ge, fill=NEG, base=-J0,
                                   pattern=[[1, 2 * NS - DS]], channel_multiplier=0))
            eng.affine_select(out=smask8, in_=smask8, compare_op=ALU.is_ge, fill=NEG, base=J0,
                              pattern=[[-1, 2 * NS - DS]], channel_multiplier=1).then_inc(s["smask8_made"], 1)
            eng.memset(onesf, 1.0).then_inc(s["consts_made"], 1)
            eng.memset(xp[:, :, 0:CW - 1], 0.0).then_inc(s["xp_edges"], 1)
            eng.iota(steps_i, pattern=[[CAP, 5]], base=0, channel_multiplier=0).then_inc(s["consts_made"], 1)
            eng.wait_ge(s["tr_ev"], 6)
            eng.dma_start(v_prompt[0, 0].rearrange("(t p) h d -> p t (h d)", p=128), tok[:, 0:2, :]).then_inc(s["out_kv"], 16)
            eng.dma_start(v_sample[0].rearrange("b q h d -> (b q) (h d)"), tok[0:NS, 2, :]).then_inc(s["out_kv"], 16)
            eng.wait_ge(s["tr_ev"], 12)
            eng.dma_start(k_prompt[0, 0].rearrange("(t p) h d -> p t (h d)", p=128), ktok[:, 0:2, :]).then_inc(s["out_kv"], 16)
            eng.dma_start(k_sample[0].rearrange("b q h d -> (b q) (h d)"), ktok[0:NS, 2, :]).then_inc(s["out_kv"], 16)
            eng.wait_ge(s["tr_ev"], 13)
            eng.dma_start(logf_prompt[0, 0].rearrange("(t p) h -> p t h", p=128), lftok[:, 0:2, :]).then_inc(s["out_states"], 16)
            eng.dma_start(logf_sample[0].rearrange("b q h -> (b q) h"), lftok[0:NS, 2, :]).then_inc(s["out_states"], 16)
            eng.wait_ge(s["tr_ev"], 19)
            eng.dma_start(h_prompt[0], strow[0:1, :]).then_inc(s["out_states"], 16)
            eng.dma_start(h_sample[0], strow[1:NR, :]).then_inc(s["out_states"], 16)
            eng.dma_start(conv_prompt[0, 0], strow[NR:NR + 3, :]).then_inc(s["out_states"], 16)
            eng.dma_start(conv_sample[0].rearrange("b j n -> (b j) n"), strow[NR + 3:36, :]).then_inc(s["out_states"], 16)
            eng.wait_ge(s["rg_done"], 1)
            eng.memset(Qbd, 0.0).then_inc(s["qbd_zero"], 1)
            eng.wait_ge(s["out_ps"], NT)
            eng.dma_start(bdn, b_down[0]).then_inc(s["late_in"], 16)
            eng.dma_start(burows, b_gate_up[0].rearrange("(g e) (m p) -> (e m) g p", g=4, p=128)).then_inc(s["late_in"], 16)
            link(eng.memset(tri, 1.0))
            eng.affine_select(out=tri, in_=tri, compare_op=ALU.is_gt, fill=0.0, base=0,
                              pattern=[[1, 128]], channel_multiplier=-1).then_inc(s["slot_made"], 1)
            eng.wait_ge(s["out_sq"], 1)
            eng.wait_ge(s["x1_made"], 1)
            eng.wait_ge(s["h2_made"], 1)
            eng.iota(sioti, pattern=[[1, CAP]], base=0, channel_multiplier=0).then_inc(s["slot_made"], 1)
            eng.iota(eioti, pattern=[[1, E]], base=0, channel_multiplier=0).then_inc(s["slot_made"], 1)
            eng.wait_ge(s["y_made"], 6)
            eng.dma_start(y_prompt[0].rearrange("(t p) n -> p t n", p=128), yrow[:, 0:2, :]).then_inc(s["out_y"], 16)
            eng.dma_start(y_sample.rearrange("b q n -> (b q) n"), yrow[0:NS, 2, :]).then_inc(s["out_y"], 16)
            eng.wait_ge(s["out_y"], 32)
            eng.wait_ge(s["out_kv"], 64)
            eng.wait_ge(s["out_states"], 96)

        def gaincol(g, kind):
            return Gm[:, g, :, :] if kind == "gain" else ada[:, NT * g:NT * g + NT, :]

        def by_sample(v):
            return v[:, :, SP_:T].rearrange("p t (b q) -> p t b q", q=DS)

        def per_sample(v):
            return v[:, :, 1:NR].unsqueeze(3).to_broadcast([128, NT, DB, DS])

        def oview(v):
            return v[:, :, S0:S0 + DB * SEG - (CW - 1)], S0

        def owin(v, start, n):
            lo = start
            return v[:, :, lo:lo + SEG * (DB - 1) + n] if DB == 1 else windows(v, lo, n)

        def windows(v, lo, n):
            width = v.shape[2]
            pad = lo + DB * SEG - width
            if pad <= 0:
                return v[:, :, lo:lo + DB * SEG].rearrange("p t (b c) -> p t b c", c=SEG)[:, :, :, 0:n]
            lo2 = lo - pad
            return v[:, :, lo2:lo2 + DB * SEG].rearrange("p t (b c) -> p t b c", c=SEG)[:, :, :, pad:pad + n]

        @block.scalar
        def _(eng):
            link = Chain(eng, s["chain_act"])
            A_ = nc.scalar.activation

            def root(v, n):
                eng.wait_ge(s["ms_made"], n)
                A_(v, v, ACT.Sqrt).then_inc(s["rs_made"], 1)

            eng.wait_ge(s["vec_made"], 1)
            A_(sigc, vec("c", NR * NT), ACT.Sigmoid).then_inc(s["csig_made"], 1)
            for t in range(NT):
                eng.wait_ge(s["xT_made"], t + 1)
                A_(gaT[:, t, :], xT[:, t, :], ACT.Square).then_inc(s["xT_sq"], 1)
            root(rs, 1)
            eng.wait_ge(s["absw_made"], 1)
            A_(t8, s8, ACT.Exp, scale=-1.0).then_inc(s["expw_made"], 1)

            def job(j):
                kind, t = JOBS[j]
                ps = B[4 + j % 4]
                eng.wait_ge(s["job_ps"], j + 1)
                if kind == "v":
                    A_(gbT[:, t, :], ps[:, 0:T], ACT.Copy).then_inc(s["job_ev"], 1)
                elif kind == "k":
                    A_(kT[:, t, :], ps[:, 0:T], ACT.Copy).then_inc(s["job_ev"], 1)
                elif kind == "q":
                    A_(qT[:, t, :], ps[:, 0:T], ACT.Copy, scale=SCALE).then_inc(s["job_ev"], 1)
                elif kind == "x":
                    link(A_(xp[:, t, CW - 1:CW - 1 + SP_], ps[:, 0:SP_], ACT.Copy))
                    A_(windows(xp, S0 + CW - 1, DS)[:, t, :, :], ps[:, SP_:T].rearrange("p (b q) -> p b q", q=DS),
                       ACT.Copy).then_inc(s["job_ev"], 1)
                elif kind == "f":
                    eng.wait_ge(s["small_in"], 64)
                    A_(lfz, ps[0:H, 0:T], ACT.Identity, bias=bfg).then_inc(s["job_ev"], 1)
                elif kind in ("r", "i"):
                    if j == LAST["q"]:
                        eng.wait_ge(s["out_kv"], 64)
                    A_((R if kind == "r" else U)[:, t, :], ps[:, 0:OW], ACT.Sigmoid,
                       bias=vec("rg_b_a" if kind == "r" else "rg_b_x")[:, t:t + 1]).then_inc(s["job_ev"], 1)
                else:
                    if kind == "gb" and t == 0:
                        eng.wait_ge(s["tr_ps"], G_K)
                    A_((gaT if kind == "ga" else gbT)[:, t, :], ps[:, 0:T], ACT.Sigmoid).then_inc(s["job_ev"], 1)

            for j in range(LAST["q"]):
                job(j)
                if j == LAST["f"] + 1:
                    eng.wait_ge(s["absw_made"], 2)
                    A_(Ssb[0:H, 0, 0:T], Ssb[0:H, 0, 0:T], ACT.Exp, scale=-1.0).then_inc(s["expw_made"], 1)
            for j in range(LAST["q"], LAST["i"] + 3):
                job(j)
            eng.wait_ge(s["decay_in"], 1)
            link(A_(A, R, ACT.Exp))
            A_(R, R, ACT.Tanh, scale=-1.0).then_inc(s["decay_out"], 1)
            for j in range(LAST["i"] + 3, LAST["i"] + 7):
                job(j)
            eng.wait_ge(s["den_made"], 1)
            A_(R, R, ACT.Sqrt, scale=2.0).then_inc(s["mult_made"], 1)
            for j in range(LAST["i"] + 7, LAST["gb"]):
                job(j)

            def exps(h):
                eng.wait_ge(s["negmax_made"], h + 1)
                P = Ssb[:, h % 3, :]
                link(A_(P[:, 0:128], P[:, 0:128], ACT.Exp, bias=nm[:, h % 3, 0:1], accum_out=rsum[:, h % 3, 0:1]))
                A_(P[:, 128:384], P[:, 128:384], ACT.Exp, bias=nm[:, h % 3, 1:2],
                   accum_out=rsum[:, h % 3, 1:2]).then_inc(s["exp_done"], 1)

            exps(0)
            exps(1)
            for h in range(H):
                eng.wait_ge(s["PT_ps"], h + 1)
                A_(PTs[:, h % 2, :], B[4 + h % 2][:, 0:384], ACT.Copy).then_inc(s["PT_ev"], 1)
                if h + 2 < H:
                    exps(h + 2)

            def keys(b):
                for g in range(4):
                    n = 4 * b + g
                    eng.wait_ge(s["KT_ps"], n + 1)
                    A_(KT[:, b % 2, 2 * g:2 * g + 2, :], B[n % 2][:, :].rearrange("p (t c) -> p t c", t=2),
                       ACT.Copy).then_inc(s["KT_ev"], 1)

            def sexps(b):
                eng.wait_ge(s["snegmax_made"], b + 1)
                A_(Ss[:, b % 2, :], Ss[:, b % 2, :], ACT.Exp, bias=sst[:, b % 2, 0:1],
                   accum_out=sst[:, b % 2, 1:2]).then_inc(s["sexp_done"], 1)

            keys(0)
            keys(1)
            sexps(0)
            for b in range(DB):
                eng.wait_ge(s["sPT_ps"], b + 1)
                link(A_(PT2[:, b % 2, 0:256], B[4 + b % 2][:, 0:256], ACT.Copy))
                A_(PT2[0:NS, b % 2, 256:384], B[4 + b % 2][0:NS, 256:384], ACT.Copy).then_inc(s["sPT_ev"], 1)
                if b + 1 < DB:
                    sexps(b + 1)
                if b + 2 < DB:
                    keys(b + 2)

            for t in range(NT):
                eng.wait_ge(s["out_read"], t + 1)
                A_(kT[:, t, :], qT[:, t, :], ACT.Square).then_inc(s["out_sq"], 1)
            root(rs2, 2)
            for half in range(2):
                eng.wait_ge(s["x1_made"], half + 1)
                if half == 0:
                    eng.wait_ge(s["rs_sq_ps"], 1)
                A_(kT[:, 4 * half:4 * half + 4, :], xT[:, 4 * half:4 * half + 4, :], ACT.Square).then_inc(s["x1_sq"], 1)
            root(rs2, 3)
            eng.wait_ge(s["topmax_made"], 1)
            A_(tope[:, :, 0:TOPK], tope[:, :, 0:TOPK], ACT.Exp).then_inc(s["topexp_made"], 1)

            def gathered(n):
                eng.wait_ge(s["gather_ps"], n)
                for i in range(2):
                    A_(XT[:, 4 * i:4 * i + 4, :], B[3 + i][:, 0:4 * SL].rearrange("p (t s) -> p t s", t=4),
                       ACT.Copy).then_inc(s["XT_made"], 1)
                eng.wait_ge(s["cT_ps"], n)
                A_(Cnext, B[5][0:SL, 0:T], ACT.Copy).then_inc(s["C_made"], 1)

            eng.wait_ge(s["tables_made"], 2)
            link(eng.memzero(YT))
            link(eng.memzero(Ccur))
            eng.sem_inc(s["YT_made"], 1)
            eng.sem_inc(s["C_moved"], 1)
            gathered(1)

            def y_rows(n):
                eng.wait_ge(s["yt_ps"], n)
                for i in range(2):
                    A_(Ysb[:, 512 * i:512 * i + 512], B[3 + i][0:SL, :], ACT.Copy).then_inc(s["Y_made"], 1)

            def pair(t, i):
                y_rows(t + 1)
                eng.wait_ge(s["glu_made"], 2 * t + 1)
                A_(sig, glu, ACT.Sigmoid, scale=ALPHA).then_inc(s["sig_made"], 1)
                eng.wait_ge(s["scatter_ps"], NT * t + NT)
                eng.wait_ge(s["C_made"], t + 1)
                A_(Ccur, Cnext, ACT.Copy).then_inc(s["C_moved"], 1)
                for half in range(2):
                    if half:
                        eng.wait_ge(s["glu_made"], 2 * t + 2)
                        A_(sig, glu, ACT.Sigmoid, scale=ALPHA).then_inc(s["sig_made"], 1)
                        eng.wait_ge(s["C_moved"], t + 2)
                        gathered(t + 2)
                    eng.wait_ge(s["dn_done"], 2 * t + (half + 2))
                    A_(YT[:, :, CAP * half:CAP * half + CAP], B[2][:, 0:NT * CAP].rearrange("p (t s) -> p t s", t=NT),
                       ACT.Copy).then_inc(s["YT_made"], 1)

            done = moe_rounds(eng, pair)
            y_rows(done + 1)
            eng.wait_ge(s["scatter_read"], NT * done + (NT + 1))
            for half in range(2):
                A_(kT[:, 4 * half:4 * half + 4, :], gbT[:, 4 * half:4 * half + 4, :], ACT.Square).then_inc(s["f_sq"], 1)
            root(rs2, 4)

        @block.vector
        def _(eng):
            link = Chain(eng, s["chain_dve"])
            V_ = nc.vector
            TTo, TS, STT = V_.tensor_tensor, V_.tensor_scalar, V_.scalar_tensor_tensor

            def log1p(acc, t, x, w, last):
                link(TS(w, t, 2.0, None, ALU.add))
                link(V_.reciprocal(w, w))
                link(TTo(x, t, w, ALU.mult))
                link(TTo(w, x, x, ALU.mult))
                link(TS(acc, w, 1.0 / 13, None, ALU.mult))
                for d in (11, 9, 7, 5, 3):
                    link(STT(acc, acc, 1.0 / d, w, ALU.add, ALU.mult))
                link(STT(acc, acc, 1.0, x, ALU.add, ALU.mult))

            def rms(dst, ps, n):
                link(TS(dst, ps, 1.0 / D, EPS, ALU.mult, ALU.add))
                V_.reciprocal(dst, dst).then_inc(s["ms_made"], 1)
                eng.wait_ge(s["rs_made"], n)

            def modulate(v, g, shift):
                G_, S_ = Gm[:, g, :, :], ada[:, NT * shift:NT * shift + NT, :]
                for t in range(NT):
                    link.later(TS(v[:, t, 0:SP_], v[:, t, 0:SP_], G_[:, t, 0:1], S_[:, t, 0:1], ALU.mult, ALU.add))
                link(TTo(by_sample(v), by_sample(v), per_sample(G_), ALU.mult))
                link(TTo(by_sample(v), by_sample(v), per_sample(S_), ALU.add))

            def ada_out(lo, hi):
                n = hi - lo
                return TTo(ada[:, lo:hi, :], B[3][:, NR * lo:NR * hi].rearrange("p (m r) -> p m r", r=NR),
                           vecT[:, V["b_ada"] + lo:V["b_ada"] + hi].unsqueeze(2).to_broadcast([128, n, NR]), ALU.add)

            def gain(g, comp, name, plus):
                return STT(Gm[:, g, :, :], ada[:, NT * comp:NT * comp + NT, :], plus,
                           vec(name).unsqueeze(2).to_broadcast([128, NT, NR]), ALU.add, ALU.mult)

            eng.wait_ge(s["ident_made"], 2)
            V_.tensor_copy(qsel.rearrange("q (h c) -> q h c", c=DS), ident[0:DS, 0:DS].unsqueeze(1).to_broadcast([DS, H, DS]))\
                .then_inc(s["qsel_made"], 1)
            eng.wait_ge(s["rows_ps"], 1)
            o = 0
            for i, n in enumerate((96, 120, 64, 96, 96)):
                link(V_.tensor_copy(vecT[:, o:o + n], B[0][:, o:o + n]))
                o += n
            eng.sem_inc(s["vec_made"], 1)
            V_.tensor_copy(smask, B[2][:, 0:2 * NS - DS]).then_inc(s["smask_made"], 1)
            for t in range(NT):
                eng.wait_ge(s["xT_ps"], t + 1)
                V_.tensor_copy(xT[:, t, :], B[4 + t % 4][:, 0:T]).then_inc(s["xT_made"], 1)
            eng.wait_ge(s["csig_made"], 1)
            TTo(vec("c", NR * NT), vec("c", NR * NT), sigc, ALU.mult).then_inc(s["c_made"], 1)
            STT(s8, vec("rg_lambda"), -1.0, vec("rg_lambda"), ALU.mult, ALU.max).then_inc(s["absw_made"], 1)
            eng.wait_ge(s["sum_ps"], 1)
            rms(rs, B[2][:, 0:T], 1)
            eng.wait_ge(s["xT_made"], NT)
            link(TTo(hT[:, :, :], xT[:, :, :], rs.unsqueeze(1).to_broadcast([128, NT, T]), ALU.mult))
            eng.wait_ge(s["ada_ps"], 1)
            link(ada_out(0, 2 * NT))
            link(gain(0, 1, "g_mix_pre", 1.0))
            modulate(hT, 0, 0)
            eng.sem_inc(s["h_made"], 1)
            eng.wait_ge(s["expw_made"], 1)
            log1p(a8, t8, sp8, s8, 1)
            link(TS(sp8, vec("rg_lambda"), -1.0, 0.0, ALU.mult, ALU.max))
            link(STT(sp8, a8, 2.0, sp8, ALU.mult, ALU.add))
            link(TS(sp8, sp8, -LRU_C, None, ALU.mult))

            def rows_out(g):
                eng.wait_ge(s["tr_ps"], g + 1)
                ps = B[g % 3]
                if g < G_LF:
                    k, half = divmod(g % 6, 2)
                    dst, n = (tok if g < G_K else ktok), TROWS[k]
                    V_.tensor_copy(dst[0:n, k, 512 * half:512 * half + 512], ps[0:n, :]).then_inc(s["tr_ev"], 1)
                elif g < G_CF:
                    for k in range(2):
                        link(V_.tensor_copy(lftok[:, k, :], ps[:, H * k:H * k + H]))
                    V_.tensor_copy(lftok[0:NS, 2, :], ps[0:NS, 2 * H:3 * H]).then_inc(s["tr_ev"], 1)
                elif g < G_ST:
                    b = 2 * (g - G_CF)
                    dst = F[:, SP_:FW].rearrange("h (b c) -> h b c", c=PAST + DS)[:, b:b + 2, 0:PAST]
                    V_.tensor_copy(dst, ps[0:H, :].rearrange("h (b c) -> h b c", b=2)).then_inc(s["tr_ev"], 1)
                else:
                    half = g - G_ST
                    V_.tensor_copy(strow[:, 512 * half:512 * half + 512], ps[0:36, :]).then_inc(s["tr_ev"], 1)

            for g in range(G_LF):
                rows_out(g)
            eng.wait_ge(s["job_ev"], LAST["x"])
            eng.wait_ge(s["xp_edges"], 1)
            for half in range(2):
                n, b0 = DB // 2, half * DB // 2
                st = vecT[:, V["conv"] + 96 * half:V["conv"] + 96 * half + 96].rearrange("p (b j t) -> p t b j", j=CW - 1, t=NT)
                link(V_.tensor_copy(xp[:, :, SP_ + CW - 1:XW].rearrange("p t (b c) -> p t b c", c=SEG)[:, :, b0:b0 + n, 0:CW - 1], st))
            for t in range(NT):
                w = vecT[:, V["conv_w"]:V["conv_w"] + CW * NT].rearrange("p (j t) -> p j t", t=NT)
                link(TS(xc[:, t, :], xp[:, t, 0:OW], w[:, 0, t:t + 1], vec("conv_b")[:, t:t + 1], ALU.mult, ALU.add))
                for j in range(1, CW):
                    ins = STT(xc[:, t, :], xp[:, t, j:j + OW], w[:, j, t:t + 1], xc[:, t, :], ALU.mult, ALU.add)
                    if j < CW - 1:
                        link(ins)
                    else:
                        ins.then_inc(s["conv_made"], 1)
            V_.tensor_copy(hsel.rearrange("k (h c) -> k h c", c=DS), ident[0:H, 0:H].unsqueeze(2).to_broadcast([H, H, DS]))\
                .then_inc(s["hsel_made"], 1)
            w_, t_, x_ = Ssb[0:H, 1, 0:T], Ssb[0:H, 0, 0:T], Ssb[0:H, 2, 0:T]
            eng.wait_ge(s["job_ev"], LAST["f"])
            STT(t_, lfz, -1.0, lfz, ALU.mult, ALU.max).then_inc(s["absw_made"], 1)
            link(V_.tensor_copy(st36[:, :, NR:NR + 3], xp[:, :, SP_:SP_ + 3]))
            link(V_.tensor_copy(st36[:, :, NR + 3:36].rearrange("p t (b j) -> p t b j", j=3),
                                xp[:, :, SP_ + CW - 1:XW].rearrange("p t (b c) -> p t b c", c=SEG)[:, :, :, DS:SEG]))
            eng.wait_ge(s["expw_made"], 2)
            acc_ = PTs[0:H, 0, 0:T]
            log1p(acc_, t_, x_, w_, 1)
            link(TS(lfz, lfz, 0.0, None, ALU.min))
            STT(lfz, acc_, -2.0, lfz, ALU.mult, ALU.add).then_inc(s["lf_made"], 1)
            rows_out(G_LF)
            eng.wait_ge(s["job_ev"], LAST["i"])
            TTo(R, R, sp8.unsqueeze(2).to_broadcast([128, NT, OW]), ALU.mult).then_inc(s["decay_in"], 1)
            link(TTo(U, U, xc, ALU.mult))
            eng.wait_ge(s["decay_out"], 1)
            link(TS(Dn, R, 1.0, None, ALU.add))
            link(V_.reciprocal(Dn, Dn))
            TTo(R, R, Dn, ALU.mult).then_inc(s["den_made"], 1)
            link(V_.memset(A[:, :, 0:1], 0.0))
            link(V_.memset(windows(A, S0 - 1, 1), 0.0))
            eng.wait_ge(s["mult_made"], 1)
            link(V_.memset(R[:, :, 0:1], 1.0))
            link(TTo(U, U, R, ALU.mult))
            link(V_.tensor_copy(windows(U, S0 - 1, 1), vec("h0", 64).rearrange("p (b t) -> p t b", t=NT).unsqueeze(3)))
            link(V_.tensor_tensor_scan(Uf, Af, Uf, 0.0, ALU.mult, ALU.add))
            link(V_.tensor_copy(st36[:, :, 0:1], U[:, :, SP_ - 1:SP_]))
            V_.tensor_copy(st36[:, :, 1:NR].unsqueeze(3), windows(U, S0 + DS - 1, 1)).then_inc(s["st_made"], 1)
            eng.wait_ge(s["job_ev"], LAST["ga"])
            link(TTo(gaT[:, :, 0:SP_], gaT[:, :, 0:SP_], U[:, :, 0:SP_], ALU.mult))
            TTo(by_sample(gaT), by_sample(gaT), windows(U, S0, DS), ALU.mult).then_inc(s["rg_done"], 1)
            eng.wait_ge(s["job_ps"], LAST["gb"])
            link(V_.tensor_copy(F[:, 0:SP_], lfz[:, 0:SP_]))
            link(V_.tensor_copy(F[:, SP_:FW].rearrange("h (b c) -> h b c", c=PAST + DS)[:, :, PAST:PAST + DS],
                                lfz[:, SP_:T].rearrange("h (b q) -> h b q", q=DS)))
            for g in range(G_CF, G_ST):
                rows_out(g)
            eng.wait_ge(s["tr_ev"], G_ST)
            eng.wait_ge(s["consts_made"], 4)
            for lo, n in [(0, SP_)] + [(SP_ + b * (PAST + DS), PAST + DS) for b in range(DB)]:
                link(V_.tensor_tensor_scan(F[:, lo:lo + n], onesf[0:H, 0:n], F[:, lo:lo + n], 0.0, ALU.mult, ALU.add))
            TS(F, F, -1.0, None, ALU.mult).then_inc(s["F_made"], 1)
            rows_out(G_ST)
            rows_out(G_ST + 1)
            eng.wait_ge(s["ada_ps"], 2)
            link(ada_out(2 * NT, 6 * NT))
            link(gain(1, 2, "g_mix_post", 0.0))
            link(gain(2, 4, "g_ffn_pre", 1.0))
            link(gain(3, 5, "g_ffn_post", 0.0))
            eng.wait_ge(s["out_states"], 96)

            def head_max(h):
                eng.wait_ge(s["scores_ps"], h + 1)
                if h >= 3:
                    eng.wait_ge(s["PT_ps"], h - 2)
                P = Ssb[:, h % 3, :]
                TTo(P, B[h % 3][:, 0:384], mask, ALU.add).then_inc(s["scores_read"], 1)
                eng.wait_ge(s["scores_read"], h + 1)
                link(V_.tensor_reduce(nm[:, h % 3, 0:1], P[:, 0:128], AX.X, ALU.max, negate=True))
                V_.tensor_reduce(nm[:, h % 3, 1:2], P[:, 128:384], AX.X, ALU.max, negate=True).then_inc(s["negmax_made"], 1)

            def head_norm(h):
                eng.wait_ge(s["exp_done"], h + 1)
                P, r_ = Ssb[:, h % 3, :], rsum[:, h % 3, :]
                link(V_.reciprocal(r_, r_))
                link(TS(P[:, 0:128], P[:, 0:128], r_[:, 0:1], None, ALU.mult))
                TS(P[:, 128:384], P[:, 128:384], r_[:, 1:2], None, ALU.mult).then_inc(s["probs_made"], 1)

            def head_out(p):
                eng.wait_ge(s["py_ps"], p + 1)
                TTo(gbT[:, p, 0:SP_], gbT[:, p, 0:SP_], B[6 + p % 2][:, 0:SP_], ALU.mult).then_inc(s["py_read"], 1)

            eng.wait_ge(s["job_ev"], LAST["gb"])
            head_max(0)
            head_max(1)
            for h in range(H):
                head_norm(h)
                if h + 2 < H:
                    head_max(h + 2)
                if h % 2 and h >= 3:
                    head_out(h // 2 - 1)
            head_out(H // 2 - 1)

            def queries(b):
                if b == 0:
                    eng.wait_ge(s["qbd_zero"], 1)
                if b >= 2:
                    eng.wait_ge(s["sscores_ps"], b - 1)
                q0 = SP_ + DS * b
                for o in (0, 1):
                    flat = Qbd[64 * o:64 * o + 64, b % 2, :, :].rearrange("d t c -> d (t c)")
                    step = 128 + 2 * DS
                    first = flat[:, o * DS:o * DS + (NT - 1) * step]
                    main = first.rearrange("d (t c) -> d t c", c=step)[:, :, 0:DS]
                    link(V_.tensor_copy(main, qT[64 * o:64 * o + 64, 0:NT - 1, q0:q0 + DS]))
                    lo = o * DS + (NT - 1) * step
                    ins = V_.tensor_copy(flat[:, lo:lo + DS], qT[64 * o:64 * o + 64, NT - 1, q0:q0 + DS])
                    if o == 0:
                        link(ins)
                    else:
                        ins.then_inc(s["qbd_made"], 1)

            def sample_max(b):
                eng.wait_ge(s["sscores_ps"], b + 1)
                P, ps = Ss[:, b % 2, :], B[2 + b % 2]
                if b >= 2:
                    eng.wait_ge(s["sPT_ps"], b - 1)
                V_.tensor_copy(P[:, 0:PAST], ps[:, 0:PAST]).then_inc(s["sscores_read"], 1)
                TTo(P[:, PAST:PAST + NS], ps[:, PAST:PAST + NS], smask[:, NS - DS - DS * b:2 * NS - DS - DS * b],
                    ALU.add).then_inc(s["sscores_read"], 1)
                eng.wait_ge(s["sscores_read"], 2 * b + 2)
                V_.tensor_reduce(sst[:, b % 2, 0:1], P, AX.X, ALU.max, negate=True).then_inc(s["snegmax_made"], 1)

            def sample_norm(b):
                eng.wait_ge(s["sexp_done"], b + 1)
                link(V_.reciprocal(sst[:, b % 2, 2:3], sst[:, b % 2, 1:2]))
                TS(Ss[:, b % 2, :], Ss[:, b % 2, :], sst[:, b % 2, 2:3], None, ALU.mult).then_inc(s["sprobs_made"], 1)

            def sample_out(b):
                eng.wait_ge(s["sy_ps"], b + 1)
                q0 = SP_ + DS * b
                y = B[6 + b % 2][:, 0:128].rearrange("p (t c) -> p t c", c=2 * DS)
                for o in (0, 1):
                    g = gbT[64 * o:64 * o + 64, :, q0:q0 + DS]
                    TTo(g, g, y[64 * o:64 * o + 64, :, DS * o:DS * o + DS], ALU.mult).then_inc(s["sy_read"], 1)

            queries(0)
            queries(1)
            sample_max(0)
            for b in range(DB):
                sample_norm(b)
                if b + 2 < DB:
                    queries(b + 2)
                if b + 1 < DB:
                    sample_max(b + 1)
                if b >= 1:
                    sample_out(b - 1)
            sample_out(DB - 1)
            eng.wait_ge(s["sy_read"], 2 * DB)
            eng.wait_ge(s["py_read"], H // 2)
            TTo(gaT[:, :, :], gaT[:, :, :], gbT[:, :, :], ALU.add).then_inc(s["merged"], 1)

            for t in range(NT):
                eng.wait_ge(s["out_ps"], t + 1)
                V_.tensor_copy(qT[:, t, :], B[4 + t % 4][:, 0:T]).then_inc(s["out_read"], 1)
            eng.wait_ge(s["rs_sq_ps"], 1)
            eng.wait_ge(s["out_read"], NT)

            def add_branch(v, rstd, g, sig_):
                for half in range(2):
                    a, z = 4 * half, 4 * half + 4
                    link(TTo(v[:, a:z, :], v[:, a:z, :], rstd.unsqueeze(1).to_broadcast([128, 4, T]), ALU.mult))
                    G_ = Gm[:, g, :, :]
                    for t in range(a, z):
                        link.later(STT(xT[:, t, 0:SP_], v[:, t, 0:SP_], G_[:, t, 0:1], xT[:, t, 0:SP_], ALU.mult, ALU.add))
                    link(TTo(by_sample(v)[:, a:z], by_sample(v)[:, a:z], per_sample(G_)[:, a:z], ALU.mult))
                    TTo(by_sample(xT)[:, a:z], by_sample(xT)[:, a:z], by_sample(v)[:, a:z], ALU.add).then_inc(sig_, 1)

            rms(rs2, B[0][:, 0:T], 2)
            add_branch(qT, rs2, 1, s["x1_made"])
            eng.wait_ge(s["rs_sq_ps"], 2)
            rms(rs2, B[1][:, 0:T], 3)
            eng.wait_ge(s["x1_made"], 2)
            link(TTo(hT[:, :, :], xT[:, :, :], rs2.unsqueeze(1).to_broadcast([128, NT, T]), ALU.mult))
            modulate(hT, 2, 3)
            eng.sem_inc(s["h2_made"], 1)
            eng.wait_ge(s["consts_made"], 4)
            link(V_.tensor_copy(steps, steps_i))
            eng.wait_ge(s["x1_sq"], 2)
            link(V_.memset(lg, 0.0))
            for g in range(6):
                eng.wait_ge(s["h2_ps"], g + 1)
                k, half = divmod(g, 2)
                V_.tensor_copy(tok[0:TROWS[k], k, 512 * half:512 * half + 512], B[2 + g % 2][0:TROWS[k], :]).then_inc(s["h2tok_made"], 1)
            eng.wait_ge(s["router_ps"], 1)
            for k in range(TT):
                link(V_.tensor_copy(lg[0:TROWS[k], k, :], B[4][0:TROWS[k], E * k:E * k + E]))
            for k in range(TT):
                link(V_.max(top[:, k, :], lg[:, k, :]))
                link(V_.max_index(topi[:, k, :], top[:, k, :], lg[:, k, :]))
            link(V_.tensor_copy(topf, topi))
            TTo(tope[:, :, 0:TOPK], top[:, :, 0:TOPK], top[:, :, 0:1].to_broadcast([128, TT, TOPK]), ALU.subtract)\
                .then_inc(s["topmax_made"], 1)
            eng.wait_ge(s["slot_made"], 3)
            link(V_.tensor_copy(slot, sioti))
            link(V_.tensor_copy(exi, eioti))
            eng.wait_ge(s["topexp_made"], 1)
            link(V_.reduce_sum(toks[:, :, 0:1], tope[:, :, 0:TOPK], AX.X))
            link(V_.reciprocal(toks[:, :, 0:1], toks[:, :, 0:1]))
            link(TTo(tope[:, :, 0:TOPK], tope[:, :, 0:TOPK], toks[:, :, 0:1].to_broadcast([128, TT, TOPK]), ALU.mult))
            exb = exi.unsqueeze(1).to_broadcast([128, TT, E])
            for j in range(TOPK):
                link(TTo(hit if j else chosen, exb, topf[:, :, j:j + 1].to_broadcast([128, TT, E]), ALU.is_equal))
                h_ = hit if j else chosen
                if j:
                    link(TTo(chosen, chosen, hit, ALU.add))
                link(TTo(hit if j else wtok, h_, tope[:, :, j:j + 1].to_broadcast([128, TT, E]), ALU.mult))
                if j:
                    link(TTo(wtok, wtok, hit, ALU.add))
            eng.sem_inc(s["chosen_made"], 1)
            eng.wait_ge(s["rank_ps"], 1)
            link(TS(rk0, chosen, 1e6, -1e6, ALU.mult, ALU.add))
            link(TTo(rk0, rk0, B[5][:, 0:TT * E].rearrange("p (t e) -> p t e", t=TT), ALU.add))
            link(V_.reduce_max(cmax, B[5][:, TT * E:TT * E + E], AX.X))
            link(TS(over, steps, cmax, None, ALU.is_lt))
            link(V_.reduce_sum(rounds_f, over, AX.X))
            V_.tensor_copy(rounds_i, rounds_f).then_inc(s["rounds_made"], 1)
            for r in range(ROUNDS + 1):
                link(TS(rank[:, :, E * r:E * r + E], rk0, float(-CAP * r), None, ALU.add))
                link(V_.tensor_copy(gate[:, :, E * r:E * r + E], wtok))
            eng.wait_ge(s["wt_ps"], 1)
            V_.tensor_copy(WT, B[6][0:E, 0:T]).then_inc(s["wt_made"], 1)
            eng.wait_ge(s["bgu_ps"], 1)
            link(V_.tensor_copy(bgu, B[7][:, :]))
            for t in range(NT):
                eng.wait_ge(s["fT_ps"], t + 1)
                V_.tensor_copy(gbT[:, t, :], B[3 + t % 2][:, 0:T]).then_inc(s["fT_made"], 1)
            eng.wait_ge(s["fT_made"], NT)
            eng.sem_inc(s["gu_read"], 1)
            eng.sem_inc(s["scatter_read"], 1)
            eng.sem_inc(s["tables_made"], 2)

            def select(n, col):
                eng.wait_ge(s["cT_ps"], n)
                shape = [128, TT, 2, CAP]
                rk, gt = (v[:, :, ds(col, 2)].unsqueeze(3).to_broadcast(shape) for v in (rank, gate))
                P4, W4 = (v.rearrange("p t (e s) -> p t e s", e=2) for v in (sel, selw))
                V_.tensor_tensor(P4, slot.unsqueeze(1).unsqueeze(1).to_broadcast(shape), rk, ALU.is_equal).then_inc(s["sel_made"], 1)
                eng.wait_ge(s["sel_made"], 2 * n + 1)
                V_.tensor_tensor(W4, P4, gt, ALU.mult).then_inc(s["sel_made"], 1)

            select(0, 0)
            PER_PAIR = 2 * 4 - 0

            def pair(t, i):
                mlink = Chain(eng, s["chain_moe"], PER_PAIR * t)
                for half in range(2):
                    n = 2 * t + half
                    eng.wait_ge(s["gu_done"], n + 1)
                    bcol = (2 * i + half) * (2 * NT)
                    bg, bl = (bgu[:, ds(bcol + o, NT)].unsqueeze(2).to_broadcast([128, NT, CAP]) for o in (0, NT))
                    mlink(TTo(glu, B[0][:, 0:NT * CAP].rearrange("p (t s) -> p t s", t=NT), bg, ALU.add))
                    TS(glu, glu, LIMIT, None, ALU.min).then_inc(s["glu_made"], 1)
                    TTo(lin, B[1][:, 0:NT * CAP].rearrange("p (t s) -> p t s", t=NT), bl, ALU.add).then_inc(s["gu_read"], 1)
                    eng.wait_ge(s["gu_read"], n + 2)
                    mlink(TS(lin, lin, LIMIT, -LIMIT, ALU.min, ALU.max))
                    eng.wait_ge(s["glu_made"], n + 1)
                    mlink(STT(lin, lin, 1.0, glu, ALU.add, ALU.mult))
                    eng.wait_ge(s["sig_made"], n + 1)
                    eng.wait_ge(s["dn_done"], n + 1)
                    TTo(act, lin, sig, ALU.mult).then_inc(s["act_made"], 1)
                    eng.wait_ge(s["act_made"], n + 1)
                    if half == 0:
                        for m in range(NT):
                            combined(t, m)
                        eng.wait_ge(s["scatter_read"], NT * t + (NT + 1))
                        select(t + 1, 2 * t + 2)
                assert mlink.n <= PER_PAIR
                while mlink.n < PER_PAIR:
                    mlink(V_.memset(over[:, 0:1], 0.0))

            def combined(t, m):
                eng.wait_ge(s["scatter_ps"], NT * t + m + 1)
                TTo(gbT[:, m, :], gbT[:, m, :], B[6 + m % 2][:, 0:T], ALU.add).then_inc(s["scatter_read"], 1)

            done = moe_rounds(eng, pair)
            for m in range(NT):
                combined(done, m)
            eng.wait_ge(s["f_sum"], 1)
            eng.wait_ge(s["scatter_read"], NT * done + (NT + 1))
            rms(rs2, B[0][:, 0:T], 4)
            add_branch(gbT, rs2, 3, s["y_ready"])
            for g in range(6):
                eng.wait_ge(s["y_ps"], g + 1)
                k, half = divmod(g, 2)
                V_.tensor_copy(yrow[0:TROWS[k], k, 512 * half:512 * half + 512], B[1 + g % 2][0:TROWS[k], :]).then_inc(s["y_made"], 1)

        @block.tensor
        def _(eng):
            mm = nc.tensor.matmul

            def tr(out, in_, rows):
                return nc.tensor.transpose(out, in_, ident[0:rows, 0:rows])

            used = [0]

            def chunk():
                c = used[0]
                used[0] += 1
                eng.wait_ge(chunk_in[c % 3], 16 * (c // 3 + 1))
                return wstage[c % 3]

            eng.wait_ge(s["ident_made"], 2)
            eng.wait_ge(s["rows_in"], 16 * 15)
            eng.wait_ge(s["smask8_made"], 1)
            o = 0
            for i, n in enumerate((96, 120, 64, 96, 96)):
                tr(B[0][:, o:o + n], vrows[0:n, i, :], n)
                o += n
            eng.wait_ge(s["qsel_made"], 1)
            mm(B[2][:, 0:2 * NS - DS], qsel, smask8,
               start=True, stop=True).then_inc(s["rows_ps"], 1)
            eng.wait_ge(s["x_in"], 32)
            for t in range(NT):
                if t >= 4:
                    eng.wait_ge(s["xT_made"], t - 3)
                for k in range(TT):
                    last = tr(B[4 + t % 4][:, 128 * k:128 * k + TROWS[k]], tok[0:TROWS[k], k, 128 * t:128 * t + 128], TROWS[k])
                last.then_inc(s["xT_ps"], 1)

            def sums(bank, sq, sq_sem, steps_):
                for t in range(NT):
                    if t in steps_:
                        eng.wait_ge(sq_sem, steps_[t])
                    last = mm(bank[:, 0:T], ones[:, :], sq[:, t, :], start=(t == 0), stop=(t == NT - 1))
                return last

            eng.wait_ge(s["smask_made"], 1)
            sums(B[2], gaT, s["xT_sq"], {t: t + 1 for t in range(NT)}).then_inc(s["sum_ps"], 1)
            c9 = vec("c", NR * NT).rearrange("p (r t) -> p t r", t=NT)

            def ada_chunk(c):
                w = chunk()
                for m in range(4):
                    for k in range(NT):
                        last = mm(B[3][:, NR * (4 * c + m):NR * (4 * c + m + 1)], w[:, k, 128 * m:128 * m + 128],
                                  c9[:, k, :], start=(k == 0), stop=(k == NT - 1))
                last.then_inc(s["chunk_free"], 1)

            eng.wait_ge(s["c_made"], 1)
            for c in range(4):
                ada_chunk(c)
            eng.wait_ge(s["chunk_free"], 4)
            eng.sem_inc(s["ada_ps"], 1)
            eng.wait_ge(s["h_made"], 1)

            def transposes(g):
                if g >= 3:
                    eng.wait_ge(s["tr_ev"], g - 2)
                ps = B[g % 3]
                if g < G_LF:
                    k, half = divmod(g % 6, 2)
                    src = gbT if g < G_K else kT
                    for i in range(4):
                        last = tr(ps[0:TROWS[k], 128 * i:128 * i + 128], src[:, 4 * half + i, 128 * k:128 * k + TROWS[k]], 128)
                elif g < G_CF:
                    eng.wait_ge(s["lf_made"], 1)
                    for k in range(TT):
                        last = tr(ps[0:TROWS[k], H * k:H * k + H], lfz[:, 128 * k:128 * k + TROWS[k]], H)
                elif g < G_ST:
                    for i in range(4):
                        last = tr(ps[0:H, 128 * i:128 * i + 128], lfc[:, 4 * (g - G_CF) + i, :], 128)
                else:
                    for i in range(4):
                        last = tr(ps[0:36, 128 * i:128 * i + 128], st36[:, 4 * (g - G_ST) + i, :], 128)
                last.then_inc(s["tr_ps"], 1)

            w = None
            for j, (kind, t) in enumerate(JOBS):
                if j >= 4:
                    eng.wait_ge(s["job_ev"], j - 3)
                ps = B[4 + j % 4]
                if kind == "f":
                    eng.wait_ge(s["small_in"], 64)
                    for k in range(NT):
                        last = mm(ps[0:H, 0:T], wf[:, k, :], hT[:, k, :], start=(k == 0), stop=(k == NT - 1))
                    last.then_inc(s["job_ps"], 1)
                elif kind in ("r", "i"):
                    if t == 0:
                        eng.wait_ge(s["rgw_in"], 64)
                    if kind == "r":
                        eng.wait_ge(s["conv_made"], t + 1)
                    mm(ps[:, 0:OW], wax[:, "ri".index(kind), t, :], xc[:, t, :], start=True, stop=True).then_inc(s["job_ps"], 1)
                else:
                    if t % 4 == 0:
                        w = chunk()
                    for k in range(NT):
                        last = mm(ps[:, 0:T], w[:, k, 128 * (t % 4):128 * (t % 4) + 128], hT[:, k, :],
                                  start=(k == 0), stop=(k == NT - 1))
                    last.then_inc(s["job_ps"], 1)
                    if t % 4 == 3:
                        eng.wait_ge(s["job_ps"], j + 1)
                        eng.sem_inc(s["chunk_free"], 1)
                if j == 12:
                    eng.wait_ge(s["job_ev"], LAST["v"])
                    for g in range(G_V, G_K):
                        transposes(g)
                if j == 20:
                    for g in range(G_K, G_LF):
                        transposes(g)
                if kind == "r" and t == NT - 1:
                    transposes(G_LF)
            eng.wait_ge(s["cachef_in"], 16 * DB * NPG)
            for g in range(G_CF, G_ST):
                transposes(g)
            for c in range(4, 8):
                ada_chunk(c)
            eng.wait_ge(s["st_made"], 1)
            for g in (G_ST, G_ST + 1):
                transposes(g)
            for c in range(8, 12):
                ada_chunk(c)
            eng.wait_ge(s["chunk_free"], len(CHUNKS) - 2)
            eng.sem_inc(s["ada_ps"], 1)

            eng.wait_ge(s["F_made"], 1)
            eng.wait_ge(s["hsel_made"], 1)
            eng.wait_ge(s["tr_ev"], G_ST + 2)
            eng.wait_ge(s["job_ev"], LAST["gb"])

            def scores(h):
                p, o = h // 2, 64 * (h % 2)
                if h >= 3:
                    eng.wait_ge(s["scores_read"], h - 2)
                row = ident[0:H, h:h + 1].to_broadcast([H, 128])
                for c, q, n in ((0, 0, 128), (128, 128, 256)):
                    mm(B[h % 3][:, c:c + n], qT[o:o + 64, p, q:q + 128], kT[o:o + 64, p, 0:n], start=True, stop=False)
                    last = mm(B[h % 3][:, c:c + n], row, F[:, 0:n], start=False, stop=True)
                last.then_inc(s["scores_ps"], 1)

            def weights(h):
                eng.wait_ge(s["probs_made"], h + 1)
                if h >= 2:
                    eng.wait_ge(s["PT_ev"], h - 1)
                for i in range(3):
                    last = tr(B[4 + h % 2][:, 128 * i:128 * i + 128], Ssb[:, h % 3, 128 * i:128 * i + 128], 128)
                last.then_inc(s["PT_ps"], 1)

            def values(h):
                p, o = h // 2, 64 * (h % 2)
                eng.wait_ge(s["PT_ev"], h + 1)
                if h % 2 == 0 and p >= 2:
                    eng.wait_ge(s["py_read"], p - 1)
                out = B[6 + p % 2][o:o + 64, :]
                mm(out[:, 0:256], tok[:, 0, HD * h:HD * h + HD], PTs[:, h % 2, 0:256], start=True, stop=False)
                last = mm(out[:, 128:256], tok[:, 1, HD * h:HD * h + HD], PTs[:, h % 2, 256:384], start=False, stop=True)
                if h % 2:
                    last.then_inc(s["py_ps"], 1)

            scores(0)
            scores(1)
            for h in range(H):
                if h + 2 < H:
                    scores(h + 2)
                if h >= 1:
                    values(h - 1)
                weights(h)
            values(H - 1)

            def keysT(b):
                eng.wait_ge(k_in[b % 2], 16 * NPG * (b // 2 + 1))
                for g in range(4):
                    n = 4 * b + g
                    if n >= 2:
                        eng.wait_ge(s["KT_ev"], n - 1)
                    for i in range(2):
                        for j in range(NPG):
                            last = tr(B[n % 2][:, PAST * i + 128 * j:PAST * i + 128 * j + 128],
                                      kv[:, b % 2, j, 128 * (2 * g + i):128 * (2 * g + i) + 128], 128)
                    last.then_inc(s["KT_ps"], 1)

            def sscores(b):
                eng.wait_ge(s["KT_ev"], 4 * b + 4)
                eng.wait_ge(s["qbd_made"], b + 1)
                if b >= 2:
                    eng.wait_ge(s["sscores_read"], 2 * (b - 1))
                ps = B[2 + b % 2]
                f0 = SP_ + b * (PAST + DS)
                for p in range(NT):
                    mm(ps[:, 0:PAST], Qbd[:, b % 2, p, :], KT[:, b % 2, p, :], start=(p == 0), stop=False)
                mm(ps[:, 0:PAST], hsel, F[:, f0:f0 + PAST], start=False, stop=True)
                for p in range(NT):
                    mm(ps[:, PAST:PAST + NS], Qbd[:, b % 2, p, :], kT[:, p, SP_:T], start=(p == 0), stop=False)
                mm(ps[:, PAST + DS * b:PAST + DS * b + DS], hsel, F[:, f0 + PAST:f0 + PAST + DS], start=False, stop=True)\
                    .then_inc(s["sscores_ps"], 1)

            def sweights(b):
                eng.wait_ge(s["sprobs_made"], b + 1)
                if b >= 2:
                    eng.wait_ge(s["sPT_ev"], b - 1)
                ps = B[4 + b % 2]
                tr(ps[:, 0:128], Ss[:, b % 2, 0:128], 128)
                tr(ps[:, 128:256], Ss[:, b % 2, 128:256], 128)
                tr(ps[0:NS, 256:384], Ss[:, b % 2, PAST:PAST + NS], 128).then_inc(s["sPT_ps"], 1)

            def svalues(b):
                eng.wait_ge(s["sPT_ev"], b + 1)
                eng.wait_ge(v_in[b % 2], 16 * NPG * (b // 2 + 1))
                if b >= 2:
                    eng.wait_ge(s["sy_read"], 2 * (b - 1))
                for p in range(NT):
                    out = B[6 + b % 2][:, 2 * DS * p:2 * DS * p + 2 * DS]
                    col = slice(2 * DS * p, 2 * DS * p + 2 * DS)
                    for j in range(NPG):
                        mm(out, kv[:, b % 2, NPG + j, 128 * p:128 * p + 128],
                           PT2[:, b % 2, 128 * j:128 * j + 128][:, col], start=(j == 0), stop=False)
                    last = mm(out, tok[0:NS, 2, 128 * p:128 * p + 128], PT2[0:NS, b % 2, 256:384][:, col], start=False, stop=True)
                last.then_inc(s["sy_ps"], 1)

            eng.wait_ge(s["py_read"], H // 2)
            keysT(0)
            sscores(0)
            keysT(1)
            for b in range(DB):
                if b + 1 < DB:
                    sscores(b + 1)
                sweights(b)
                svalues(b)
                if b + 2 < DB:
                    keysT(b + 2)
            eng.wait_ge(s["sy_ps"], DB)
            eng.sem_inc(s["dn_free"], 2)

            eng.wait_ge(s["merged"], 1)
            for t in range(NT):
                if t % 4 == 0:
                    w = chunk()
                if t >= 4:
                    eng.wait_ge(s["out_read"], t - 3)
                for k in range(NT):
                    last = mm(B[4 + t % 4][:, 0:T], w[:, k, 128 * (t % 4):128 * (t % 4) + 128], gaT[:, k, :],
                              start=(k == 0), stop=(k == NT - 1))
                last.then_inc(s["out_ps"], 1)
            eng.wait_ge(s["out_ps"], NT)
            eng.sem_inc(s["gu_free"], 4)
            sums(B[0], kT, s["out_sq"], {t: t + 1 for t in range(NT)}).then_inc(s["rs_sq_ps"], 1)
            sums(B[1], kT, s["x1_sq"], {0: 1, 4: 2}).then_inc(s["rs_sq_ps"], 1)
            eng.wait_ge(s["h2_made"], 1)
            for g in range(6):
                k, half = divmod(g, 2)
                if g >= 2:
                    eng.wait_ge(s["h2tok_made"], g - 1)
                for i in range(4):
                    last = tr(B[2 + g % 2][0:TROWS[k], 128 * i:128 * i + 128], hT[:, 4 * half + i, 128 * k:128 * k + TROWS[k]], 128)
                last.then_inc(s["h2_ps"], 1)
            for k in range(TT):
                n = TROWS[k]
                ps = B[4][0:n, E * k:E * k + E]
                for t in range(NT):
                    mm(ps, hT[:, t, 128 * k:128 * k + n], wr[:, t, :], start=(t == 0), stop=False)
                last = mm(ps, ones[0:1, 0:n], brow, start=False, stop=True)
            last.then_inc(s["router_ps"], 1)
            eng.wait_ge(s["late_in"], 32)
            for g in range(4):
                last = tr(B[7][:, 128 * g:128 * g + 128], burows[:, g, :], 128)
            last.then_inc(s["bgu_ps"], 1)
            eng.wait_ge(s["chosen_made"], 1)
            eng.wait_ge(s["slot_made"], 1)
            for k in range(TT + 1):
                ps = B[5][:, E * k:E * k + E]
                for j in range(min(k, TT - 1) + 1):
                    n = TROWS[j]
                    last = mm(ps, (tri if j == k else ones)[0:n, :], chosen[0:n, j, :], start=(j == 0), stop=(j == min(k, TT - 1)))
            last.then_inc(s["rank_ps"], 1)
            for k in range(TT):
                last = tr(B[6][0:E, 128 * k:128 * k + TROWS[k]], wtok[0:TROWS[k], k, :], TROWS[k])
            last.then_inc(s["wt_ps"], 1)
            eng.wait_ge(s["wt_made"], 1)
            for t in range(NT):
                if t >= 2:
                    eng.wait_ge(s["fT_made"], t - 1)
                mm(B[3 + t % 2][:, 0:T], bdn[:, 128 * t:128 * t + 128], WT, start=True, stop=True).then_inc(s["fT_ps"], 1)
            eng.wait_ge(s["tables_made"], 2)

            def gather(n):
                eng.wait_ge(s["sel_made"], 2 * n)
                for m in range(NT):
                    out = B[3 + m // 4][:, SL * (m % 4):SL * (m % 4) + SL]
                    for k in range(TT):
                        r = TROWS[k]
                        last = mm(out, tok[0:r, k, 128 * m:128 * m + 128], sel[0:r, k, :], start=(k == 0), stop=(k == TT - 1))
                last.then_inc(s["gather_ps"], 1)
                for k in range(TT):
                    r = TROWS[k]
                    last = tr(B[5][0:SL, 128 * k:128 * k + r], selw[0:r, k, :], r)
                last.then_inc(s["cT_ps"], 1)

            def combine(n):
                eng.wait_ge(s["YT_made"], 2 * n + 1)
                for m in range(NT):
                    last = tr(B[3 + m // 4][0:SL, 128 * (m % 4):128 * (m % 4) + 128], YT[:, m, :], 128)
                last.then_inc(s["yt_ps"], 1)
                eng.wait_ge(s["C_moved"], n + 1)
                for m in range(NT):
                    eng.wait_ge(s["Y_made"], 2 * n + (1 if m < 4 else 2))
                    eng.wait_ge(s["scatter_read"], NT * n + (m if m >= 2 else 1))
                    mm(B[6 + m % 2][:, 0:T], Ysb[:, 128 * m:128 * m + 128], Ccur, start=True, stop=True).then_inc(s["scatter_ps"], 1)

            eng.sem_inc(s["dn_done"], 1)
            gather(1)

            def pair(t, i):
                for half in range(2):
                    n = 2 * t + half
                    if half == 0:
                        eng.wait_ge(s["XT_made"], 2 * t + 2)
                    eng.wait_ge(s["gu_read"], n + 1)
                    for c in range(4):
                        eng.wait_ge(gu_in[c], 32 * t + 16 * (half + 1))
                        for a in range(2):
                            k = 2 * c + a
                            for m in range(2 * NT):
                                last = mm(B[m // NT][:, CAP * (m % NT):CAP * (m % NT) + CAP], wgu[:, c, a, 128 * m:128 * m + 128],
                                          XT[:, k, CAP * half:CAP * half + CAP], start=(k == 0 and m % NT == 0),
                                          stop=(k == NT - 1 and m % NT == NT - 1), skip_group_check=True)
                        if c < 3:
                            last.then_inc(s["gu_free"], 1)
                        else:
                            last.then_inc(s["gu_done"], 1)
                            eng.wait_ge(s["gu_done"], n + 1)
                            eng.sem_inc(s["gu_free"], 1)
                    if half == 0:
                        combine(t)
                    else:
                        eng.wait_ge(s["C_made"], t + 1)
                        gather(t + 2)
                    eng.wait_ge(s["act_made"], n + 1)
                    eng.wait_ge(s["YT_made"], n + 1)
                    for c in range(2):
                        eng.wait_ge(dn_in[c], 32 * t + 16 * (half + 1))
                        for a in range(4):
                            k = 4 * c + a
                            for m in range(NT):
                                last = mm(B[2][:, CAP * m:CAP * m + CAP], wdn[:, c, a, 128 * m:128 * m + 128], act[:, k, :],
                                          start=(k == 0 and m == 0), stop=(k == NT - 1 and m == NT - 1), skip_group_check=True)
                        if c < 1:
                            last.then_inc(s["dn_free"], 1)
                        else:
                            last.then_inc(s["dn_done"], 1)
                            eng.wait_ge(s["dn_done"], n + 2)
                            eng.sem_inc(s["dn_free"], 1)

            done = moe_rounds(eng, pair)
            combine(done)
            sums(B[0], kT, s["f_sq"], {0: 1, 4: 2}).then_inc(s["f_sum"], 1)
            for g in range(6):
                k, half = divmod(g, 2)
                eng.wait_ge(s["y_ready"], half + 1 if g < 2 else 2)
                if g >= 2:
                    eng.wait_ge(s["y_made"], g - 1)
                for i in range(4):
                    last = tr(B[1 + g % 2][0:TROWS[k], 128 * i:128 * i + 128], xT[:, 4 * half + i, 128 * k:128 * k + TROWS[k]], 128)
                last.then_inc(s["y_ps"], 1)


_INS = ['x_prompt', 'x_sample', 'cache_k', 'cache_v', 'cache_logf', 'state_conv', 'state_h', 'page_table',
        'c_prompt', 'c_sample', 'w_ada', 'b_ada', 'g_mix_pre', 'g_mix_post', 'w_in', 'b_forget',
        'conv_w', 'conv_b', 'rg_w_a', 'rg_b_a', 'rg_w_x', 'rg_b_x', 'rg_lambda', 'w_out',
        'g_ffn_pre', 'g_ffn_post', 'w_router', 'b_router', 'w_gate_up', 'b_gate_up', 'w_down', 'b_down']


def kernel(**inputs):
    import numpy as _np
    import concourse.bacc as _bacc
    from concourse import mybir as _mybir
    from concourse.bass_utils import run_bass_kernel_spmd as _run

    nc = _bacc.Bacc("TRN2", target_bir_lowering=False, num_devices=1)
    arrays, args = {}, []
    for name in _INS:
        a = _np.ascontiguousarray(inputs[name])
        arrays[f"in_{name}_dram"] = a
        args.append(nc.dram_tensor(f"in_{name}_dram", a.shape, _mybir.dt.from_np(a.dtype), kind="ExternalInput").ap())
    xs, xd = inputs['x_prompt'].shape, inputs['x_sample'].shape
    heads, hd = inputs['cache_k'].shape[3:]
    conv = inputs['state_conv'].shape
    outs = [xs, xd]
    for n, m in ((xs[0], xs[1]), (xd[0], xd[1])):
        outs += [(1, n, m, heads, hd), (1, n, m, heads, hd), (1, n, m, heads), (1, n, conv[2], conv[3]), (1, n, conv[3])]
    for i, shape in enumerate(outs):
        args.append(nc.dram_tensor(f"out_{i}_dram", shape, _mybir.dt.float32, kind="ExternalOutput").ap())
    hybrid_layer(nc, *args)
    r = _run(nc, [arrays], core_ids=[0])
    return tuple(r.results[0][f"out_{i}_dram"] for i in range(len(outs)))
```

```python
from contextlib import ExitStack

import concourse.bass as bass
from concourse import mybir

CAP = 64


class Chain:

    def __init__(self, eng, sem, base=None):
        self.eng, self.sem, self.base, self.n = eng, sem, base, 0

    def later(self, ins):
        ins.then_inc(self.sem, 1)
        self.n += 1

    def __call__(self, ins):
        self.later(ins)
        self.eng.wait_ge(self.sem, self.n if self.base is None else self.base + self.n)


def hybrid_layer(nc, x_prompt, x_sample, cache_k, cache_v, cache_logf, state_conv, state_h, page_table,
                 c_prompt, c_sample, w_ada, b_ada, g_mix_pre, g_mix_post, w_in, b_forget,
                 conv_w, conv_b, rg_w_a, rg_b_a, rg_w_x, rg_b_x, rg_lambda, w_out,
                 g_ffn_pre, g_ffn_post, w_router, b_router, w_gate_up, b_gate_up, w_down, b_down,
                 y_prompt, y_sample, k_prompt, v_prompt, logf_prompt, conv_prompt, h_prompt,
                 k_sample, v_sample, logf_sample, conv_sample, h_sample):
    f32, i32, u32 = mybir.dt.float32, mybir.dt.int32, mybir.dt.uint32
    ALU, ACT, AX = mybir.AluOpType, mybir.ActivationFunctionType, mybir.AxisListType
    ds = bass.ds

    D = x_prompt.shape[2]
    NT = D // 128
    SP_, DB, DS = x_prompt.shape[1], x_sample.shape[0], x_sample.shape[1]
    NS = DB * DS
    T = SP_ + NS
    TT = 3
    TROWS = [128, 128, NS]
    NR = 1 + DB
    H, HD = cache_k.shape[3], cache_k.shape[4]
    PG, NPOOL, NPG = cache_k.shape[2], cache_k.shape[1], page_table.shape[1]
    PAST = PG * NPG
    E, TOPK = w_router.shape[2], 4
    CW = conv_w.shape[1]
    SEG = CW - 1 + DS
    XW = CW - 1 + SP_ + DB * SEG
    OW = XW - (CW - 1)
    S0 = SP_ + CW - 1
    FW = SP_ + DB * (PAST + DS)
    EPS, LIMIT, ALPHA, SCALE, LRU_C = 1e-6, 7.0, 1.702, float(HD) ** -0.5, 8.0
    NEG = -1e30
    PAIRS, ROUNDS, SL = E // 2, -(-T // CAP), 2 * CAP
    RCOLS = E * (ROUNDS + 1)

    ctx = ExitStack()
    with ctx:
        def sb(name, shape, dt=f32):
            return ctx.enter_context(nc.sbuf_tensor(name, shape, dt))

        def sem(name):
            return ctx.enter_context(nc.semaphore(name))

        wgu = sb("wgu", [128, 4, 2, 2 * D])
        wdn = sb("wdn", [128, 4, 2, D])
        xT = sb("xT", [128, NT, T])
        hT = sb("hT", [128, NT, T])
        qT = sb("qT", [128, NT, T])
        kT = sb("kT", [128, NT, T])
        gaT = sb("gaT", [128, NT, T])
        gbT = sb("gbT", [128, NT, T])
        tok = sb("tok", [128, TT, D])
        work = sb("work", [128, 8280])
        ident = sb("ident", [128, 128])
        ones = sb("ones", [128, 128])
        ada = sb("ada", [128, 6 * NT, NR])
        Gm = sb("Gm", [128, 4, NT, NR])
        vecT = sb("vecT", [128, 472])
        wr = sb("wr", [128, NT, E])
        tiny = sb("tiny", [128, 136])

        wstage = [wgu[:, s, :, :].rearrange("p a n -> p (a n)").rearrange("p (k n) -> p k n", k=NT) for s in range(3)]
        fr = wgu[:, 3, :, :].rearrange("p a n -> p (a n)")
        Ssb = fr[:, 0:1152].rearrange("p (s n) -> p s n", s=3)
        PTs = fr[:, 1152:1920].rearrange("p (s n) -> p s n", s=2)
        mask = fr[:, 1920:2304]
        smask = fr[:, 2304:2304 + 2 * NS - DS]
        lfc = fr[:, 2432:2688].rearrange("p (g h) -> p g h", h=H)
        wf = fr[:, 2688:2816].rearrange("p (k h) -> p k h", h=H)
        onesf = fr[:, 2816:2816 + PAST + DS]
        st36 = fr[:, 3080:3080 + NT * 36].rearrange("p (t c) -> p t c", c=36)
        rs = fr[:, 3368:3688]
        lfz = fr[0:H, 3688:4008]
        lftok = fr[:, 4008:4056].rearrange("p (t h) -> p t h", h=H)
        rg = wdn[:, :, :, :].rearrange("p a k n -> p (a k n)")
        xc = rg[:, 0:NT * OW].rearrange("p (t c) -> p t c", t=NT)
        R = rg[:, NT * OW:2 * NT * OW].rearrange("p (t c) -> p t c", t=NT)
        wax = rg[:, 2 * NT * OW:2 * NT * OW + 2048].rearrange("p (g t c) -> p g t c", g=2, t=NT)
        kv = rg.rearrange("p (s g n) -> p s g n", s=2, g=4)

        NX, NO = NT * XW, NT * OW
        xp = work[:, 0:NX].rearrange("p (t c) -> p t c", t=NT)
        Dn = work[:, 0:NO].rearrange("p (t c) -> p t c", t=NT)
        Af = work[:, NX:NX + NO]
        Uf = work[:, NX + NO:NX + 2 * NO]
        A = Af.rearrange("p (t c) -> p t c", t=NT)
        U = Uf.rearrange("p (t c) -> p t c", t=NT)
        ktok = work[:, NX:NX + TT * D].rearrange("p (t n) -> p t n", t=TT)
        vrows = work[:, 5900:6540].rearrange("p (g n) -> p g n", g=5)
        strow = fr[0:36, 0:D]
        KT = work[:, 0:5120].rearrange("p (s t c) -> p s t c", s=2, t=NT)
        QB = 6 * DS
        Qbd = work[:, 5120:5120 + 2 * QB * NT].rearrange("p (s c) -> p s c", s=2)
        Ss = work[:, 5888:6528].rearrange("p (s c) -> p s c", s=2)
        PT2 = work[:, 6528:7296].rearrange("p (s c) -> p s c", s=2)
        Ym = work[:, 7296:7808].rearrange("p (s c) -> p s c", s=2)
        fold8 = work[:, 7808:7840]
        at = [0]

        def carve(n, area=work, limit=8280):
            at[0] += n
            assert at[0] <= limit
            return area[:, at[0] - n:at[0]]

        XT = carve(NT * SL).rearrange("p (t s) -> p t s", t=NT)
        glu = carve(D)
        lin = carve(D)
        sig = carve(D)
        actT = carve(NT * SL).rearrange("p (t s) -> p t s", t=NT)
        Ysb = carve(D)[0:SL, :]
        sel = carve(TT * SL).rearrange("p (t s) -> p t s", t=TT)
        selw = carve(TT * SL).rearrange("p (t s) -> p t s", t=TT)
        Cnext = carve(T)[0:SL, :]
        Ccur = carve(T)[0:SL, :]
        esel = carve(SL)[0:E, :]
        tri = carve(128)
        slot = carve(CAP)
        yrow = work[:, 0:TT * D].rearrange("p (t n) -> p t n", t=TT)
        qf = qT[:, :, :].rearrange("p t n -> p (t n)")
        kf = kT[:, :, :].rearrange("p t n -> p (t n)")
        gaf = gaT[:, :, :].rearrange("p t n -> p (t n)")
        rank = qf[:, 0:TT * RCOLS].rearrange("p (t c) -> p t c", t=TT)
        gate = qf[:, TT * RCOLS:2 * TT * RCOLS].rearrange("p (t c) -> p t c", t=TT)
        lg = kf[:, 0:96].rearrange("p (t e) -> p t e", t=TT)
        top = kf[:, 96:120].rearrange("p (t e) -> p t e", t=TT)
        topi = kf[:, 120:144].bitcast(u32).rearrange("p (t e) -> p t e", t=TT)
        topf = kf[:, 144:168].rearrange("p (t e) -> p t e", t=TT)
        tope = kf[:, 168:192].rearrange("p (t e) -> p t e", t=TT)
        toks = kf[:, 192:216].rearrange("p (t e) -> p t e", t=TT)
        hit = kf[:, 216:312].rearrange("p (t e) -> p t e", t=TT)
        chosen = kf[:, 312:408].rearrange("p (t e) -> p t e", t=TT)
        wtok = kf[:, 408:504].rearrange("p (t e) -> p t e", t=TT)
        rk0 = kf[:, 504:600].rearrange("p (t e) -> p t e", t=TT)
        exi = kf[:, 600:600 + E]
        WT = kf[0:E, 640:640 + T]
        bdn = gaf[0:E, 0:D]
        bgu = hT[0:E, :, :].rearrange("p t n -> p (t n)")[:, 0:2 * D]
        rs2 = gaf[:, 1600:1600 + T]
        F = hT[0:H, :, :].rearrange("p t n -> p (t n)")[:, 0:FW]

        def few(a, n, parts=128):
            return tiny[0:parts, a:a + n]

        sp8, t8, s8, a8 = few(0, 8), few(8, 8), few(16, 8), few(24, 8)
        bfg = few(32, 1, H)
        brow = few(33, E, 1)
        nm = few(66, 6).rearrange("p (s n) -> p s n", s=3)
        rsum = few(72, 6).rearrange("p (s n) -> p s n", s=3)
        sst = few(78, 6).rearrange("p (s n) -> p s n", s=2)
        cmax, rounds_f, over = few(84, 1), few(85, 1), few(86, 5)
        rounds_i = few(92, 1).bitcast(i32)
        steps_i = few(94, 5).bitcast(i32)
        steps = few(100, 5)
        ptab = few(106, 16, 1).bitcast(i32)
        fold9 = few(122, NR)
        hm4 = few(131, 4)
        silu_c = PTs[:, 1, 0:256].rearrange("p (t r) -> p t r", t=NT)
        adarow = qf[:, 0:4 * 512].rearrange("p (s n) -> p s n", s=4)
        sigc = kf[:, 0:NR * NT]
        smask8 = kf[0:DS, 1200:1200 + 2 * NS - DS]
        qsel = kf[0:DS, 1400:1400 + H * DS]
        sioti = kf[:, 1000:1000 + CAP].bitcast(i32)
        eioti = kf[:, 1064:1064 + E].bitcast(i32)

        B = [ctx.enter_context(nc.psum_tensor(f"bank{i}", [128, 512], f32)) for i in range(8)]

        V = dict(g_mix_pre=0, g_mix_post=8, g_ffn_pre=16, g_ffn_post=24, conv_b=32, rg_b_a=40, rg_b_x=48,
                 rg_lambda=56, conv_w=64, b_ada=96, c=144, h0=216, conv=280)

        hsel = vecT[0:H, 280:280 + H * DS]

        def vec(name, n=NT):
            return vecT[:, V[name]:V[name] + n]

        names = """fold8_made fold_ps silu_zeroed tailk_made sv_ps sv_made smask8_made qsel_made hsel_made smask_made
            consts_made ident_made x_in rows_in small_in pages_in cachef_in rgw_zeroed rgw_in rows_ps vec_made
            csig_made c_made xT_ps xT_made xT_sq sum_ps ms_made rs_made ada_ps h_made chunk_free job_ps job_ev
            tr_ps tr_ev xp_edges conv_made absw_made expw_made lf_made decay_in decay_out den_made mult_made
            st_made rg_done F_made scores_ps scores_read negmax_made exp_done probs_made PT_ps PT_ev py_ps
            py_read qbd_zero qbd_made KT_ps KT_ev sscores_ps sscores_read snegmax_made sexp_done sprobs_made
            sPT_ps sPT_ev sy_ps sy_read merged out_ps out_read out_sq rs_sq_ps x1_made x1_sq h2_made h2_ps
            h2tok_made late_in bgu_in slot_made router_ps topmax_made topexp_made chosen_made rank_ps wt_ps
            wt_made fT_ps fT_made tables_made rounds_made gu_free dn_free esel_made gu_done glu_made sig_made
            lin_made act_made aT_ps aT_made dn_done Y_made sel_made gather_ps XT_made cT_ps C_made C_moved
            scatter_ps scatter_read f_sq f_sum y_ready y_ps y_made chain_dve chain_act chain_pool out_kv
            out_states out_y""".split()
        s = {n: sem(n) for n in names}
        chunk_in = [sem(f"chunk_in{i}") for i in range(3)]
        k_in = [sem(f"k_in{i}") for i in range(2)]
        v_in = [sem(f"v_in{i}") for i in range(2)]
        gu_in = [sem(f"gu_in{i}") for i in range(4)]
        dn_in = [sem(f"dn_in{i}") for i in range(4)]

        adav = w_ada[0].rearrange("(k p) n -> p k n", p=128)
        winv = w_in[0].rearrange("(k p) n -> p k n", p=128)
        woutv = w_out[0].rearrange("(k p) n -> p k n", p=128)
        FCOL = 4 * D
        ZCOL = dict(x=0, q=D, k=2 * D, v=3 * D, ga=FCOL + H, gb=FCOL + H + D)
        JOBS = [("a", c) for c in range(4)]
        extra = [[4], [5], [6], [7], [8], [9, 10, 11]]
        for i, z in enumerate("vvkkxx"):
            JOBS += [(z, 4 * (i % 2) + t) for t in range(4)] + [("a", c) for c in extra[i]]
        JOBS += [("f", 0)] + [("q", t) for t in range(NT)]
        JOBS += [("r", t) for t in range(NT)] + [("i", t) for t in range(NT)]
        JOBS += [("ga", t) for t in range(NT)] + [("gb", t) for t in range(NT)]
        CHUNKS = []
        for kind, t in JOBS:
            if kind == "a":
                CHUNKS.append(adav[:, :, 512 * t:512 * t + 512])
            elif kind in ZCOL and t % 4 == 0:
                CHUNKS.append(winv[:, :, ZCOL[kind] + 128 * t:ZCOL[kind] + 128 * t + 512])
        CHUNKS += [woutv[:, :, 512 * i:512 * i + 512] for i in range(2)]
        LAST = {k: max(i for i, j in enumerate(JOBS) if j[0] == k) + 1 for k in "a v k x f q r i ga gb".split()}
        G_V, G_K, G_LF, G_CF, G_ST = 0, 6, 12, 13, 17
        block = ctx.enter_context(nc.Block())

        def page(eng, i):
            return eng.value_load(ptab[0:1, i:i + 1], min_val=0, max_val=NPOOL - 1)

        def moe_rounds(eng, pair):
            with eng.Fori(0, PAIRS) as i:
                pair(i, i)
            eng.wait_ge(s["rounds_made"], 1)
            n = eng.value_load(rounds_i[0:1, :], min_val=1, max_val=ROUNDS)
            with eng.Fori(1, ROUNDS) as r:
                with eng.If(r < n):
                    with eng.Fori(0, PAIRS) as i:
                        pair(r * PAIRS + i, i)
            return n * PAIRS

        @block.sync
        def _(eng):
            for name, src in (("x", (x_prompt[0].rearrange("(t p) n -> p t n", p=128), tok[:, 0:2, :])),
                              ("s", (x_sample.rearrange("b q n -> (b q) n"), tok[0:NS, 2, :]))):
                eng.dma_start(src[1], src[0]).then_inc(s["x_in"], 16)

            def tiles(v, o="(t p)"):
                return v.rearrange("o (t p) -> (o t) p", p=128)

            for at_, v in ((0, g_mix_pre), (8, g_mix_post), (16, g_ffn_pre), (24, g_ffn_post), (32, conv_b),
                           (40, rg_b_a), (48, rg_b_x), (56, rg_lambda), (64, conv_w[0])):
                rows = v.shape[0] * NT
                eng.dma_start(vrows[at_:at_ + rows, 0, :], tiles(v)).then_inc(s["rows_in"], 16)
            for at_, v in ((0, b_ada), (48, c_prompt), (56, c_sample)):
                rows = v.shape[0] * v.shape[1] // 128
                eng.dma_start(vrows[at_:at_ + rows, 1, :], tiles(v)).then_inc(s["rows_in"], 16)
            eng.dma_start(vrows[0:64, 2, :], tiles(state_h[0])).then_inc(s["rows_in"], 16)
            scv = state_conv[0].rearrange("b j (t p) -> (b j t) p", p=128)
            for i in range(2):
                eng.dma_start(vrows[0:96, 3 + i, :], scv[96 * i:96 * i + 96, :]).then_inc(s["rows_in"], 16)

            def chunk(c):
                if c >= 3:
                    eng.wait_ge(s["chunk_free"], c - 2)
                eng.dma_start(wstage[c % 3], CHUNKS[c]).then_inc(chunk_in[c % 3], 16)

            for c in range(10):
                chunk(c)
            eng.dma_start(ptab, page_table.rearrange("(o b) g -> o (b g)", o=1)).then_inc(s["pages_in"], 16)
            eng.dma_start(wf, winv[:, :, FCOL:FCOL + H]).then_inc(s["small_in"], 16)
            eng.dma_start(bfg, b_forget.rearrange("o h -> h o")).then_inc(s["small_in"], 16)
            eng.dma_start(wr[:, :, :], w_router[0].rearrange("(k p) e -> p k e", p=128)).then_inc(s["small_in"], 16)
            eng.dma_start(brow, b_router).then_inc(s["small_in"], 16)
            eng.wait_ge(s["rgw_zeroed"], 1)
            for g, w in enumerate((rg_w_a, rg_w_x)):
                wv = w[0].rearrange("(t two) c d -> two c t d", two=2)
                for two in range(2):
                    o = 64 * two
                    eng.dma_start(wax[o:o + 64, g, :, o:o + 64], wv[two]).then_inc(s["rgw_in"], 16)
            eng.wait_ge(s["pages_in"], 16)
            for i in range(DB * NPG):
                eng.dma_start(lfc[:, i, :], cache_logf[0, ds(page(eng, i), 1), :, :].rearrange("o p h -> (o p) h"))\
                    .then_inc(s["cachef_in"], 16)
            for c in range(10, len(CHUNKS)):
                chunk(c)
            eng.wait_ge(s["rg_done"], 1)
            for b in range(DB):
                for g, c, in_ in ((0, cache_k, k_in), (NPG, cache_v, v_in)):
                    if b >= 2 and g == 0:
                        eng.wait_ge(s["KT_ps"], 4 * (b - 1))
                    if b >= 2 and g:
                        eng.wait_ge(s["sy_ps"], b - 1)
                    for i in range(NPG):
                        eng.dma_start(kv[:, b % 2, g + i, :],
                                      c[0, ds(page(eng, NPG * b + i), 1), :, :, :].rearrange("o p h d -> (o p) (h d)"))\
                            .then_inc(in_[b % 2], 16)

            guv = w_gate_up[0].rearrange("e (k p) n -> k p e n", p=128)
            dnv = w_down[0].rearrange("e (k p) n -> k p e n", p=128)

            def gate_up(t, i, lo, hi):
                for k in range(lo, hi):
                    eng.wait_ge(s["gu_free"], NT * t + (k + 1))
                    eng.dma_start(wgu[:, k % 4, :, :], guv[k, :, ds(2 * i, 2), :]).then_inc(gu_in[k % 4], 16)

            def down(t, i, lo, hi):
                for k in range(lo, hi):
                    eng.wait_ge(s["dn_free"], NT * t + (k + 1))
                    eng.dma_start(wdn[:, k % 4, :, :], dnv[k, :, ds(2 * i, 2), :]).then_inc(dn_in[k % 4], 16)

            def a_round(base):
                gate_up(base, 0, 0, 4)
                down(base, 0, 0, 4)
                with eng.Fori(0, PAIRS - 1) as i:
                    gate_up(base + i, i, 4, NT)
                    gate_up(base + (i + 1), i + 1, 0, 4)
                    down(base + i, i, 4, NT)
                    down(base + (i + 1), i + 1, 0, 4)
                gate_up(base + (PAIRS - 1), PAIRS - 1, 4, NT)
                down(base + (PAIRS - 1), PAIRS - 1, 4, NT)

            a_round(0)
            eng.wait_ge(s["rounds_made"], 1)
            n = eng.value_load(rounds_i[0:1, :], min_val=1, max_val=ROUNDS)
            with eng.Fori(1, ROUNDS) as r:
                with eng.If(r < n):
                    a_round(r * PAIRS)

        @block.gpsimd
        def _(eng):
            link = Chain(eng, s["chain_pool"])
            link(eng.memset(ident[:, :], 0.0))
            eng.affine_select(out=ident[:, :], in_=ident[:, :], compare_op=ALU.not_equal, fill=1.0, base=0,
                              pattern=[[-1, 128]], channel_multiplier=1).then_inc(s["ident_made"], 1)
            eng.memset(ones[:, :], 1.0).then_inc(s["ident_made"], 1)
            eng.memset(silu_c, 0.0).then_inc(s["silu_zeroed"], 1)
            eng.memset(wax, 0.0).then_inc(s["rgw_zeroed"], 1)
            link(eng.memset(mask, 0.0))
            for o in (0, 256):
                eng.affine_select(out=mask[:, o:o + 128], in_=mask[:, o:o + 128], compare_op=ALU.is_ge, fill=NEG,
                                  base=0, pattern=[[-1, 128]], channel_multiplier=1).then_inc(s["consts_made"], 1)
            J0 = NS - DS
            link(eng.memset(smask8, 0.0))
            link(eng.affine_select(out=smask8, in_=smask8, compare_op=ALU.is_ge, fill=NEG, base=-J0,
                                   pattern=[[1, 2 * NS - DS]], channel_multiplier=0))
            eng.affine_select(out=smask8, in_=smask8, compare_op=ALU.is_ge, fill=NEG, base=J0,
                              pattern=[[-1, 2 * NS - DS]], channel_multiplier=1).then_inc(s["smask8_made"], 1)
            eng.memset(onesf, 1.0).then_inc(s["consts_made"], 1)
            eng.memset(xp[:, :, 0:CW - 1], 0.0).then_inc(s["xp_edges"], 1)
            eng.iota(steps_i, pattern=[[CAP, 5]], base=0, channel_multiplier=0).then_inc(s["consts_made"], 1)
            eng.wait_ge(s["tr_ev"], 6)
            eng.dma_start(v_prompt[0, 0].rearrange("(t p) h d -> p t (h d)", p=128), tok[:, 0:2, :]).then_inc(s["out_kv"], 16)
            eng.dma_start(v_sample[0].rearrange("b q h d -> (b q) (h d)"), tok[0:NS, 2, :]).then_inc(s["out_kv"], 16)
            eng.wait_ge(s["tr_ev"], 12)
            eng.dma_start(k_prompt[0, 0].rearrange("(t p) h d -> p t (h d)", p=128), ktok[:, 0:2, :]).then_inc(s["out_kv"], 16)
            eng.dma_start(k_sample[0].rearrange("b q h d -> (b q) (h d)"), ktok[0:NS, 2, :]).then_inc(s["out_kv"], 16)
            eng.wait_ge(s["tr_ev"], 13)
            eng.dma_start(logf_prompt[0, 0].rearrange("(t p) h -> p t h", p=128), lftok[:, 0:2, :]).then_inc(s["out_states"], 16)
            eng.dma_start(logf_sample[0].rearrange("b q h -> (b q) h"), lftok[0:NS, 2, :]).then_inc(s["out_states"], 16)
            eng.wait_ge(s["tr_ev"], 19)
            eng.dma_start(h_prompt[0], strow[0:1, :]).then_inc(s["out_states"], 16)
            eng.dma_start(h_sample[0], strow[1:NR, :]).then_inc(s["out_states"], 16)
            eng.dma_start(conv_prompt[0, 0], strow[NR:NR + 3, :]).then_inc(s["out_states"], 16)
            eng.dma_start(conv_sample[0].rearrange("b j n -> (b j) n"), strow[NR + 3:36, :]).then_inc(s["out_states"], 16)
            eng.wait_ge(s["rg_done"], 1)
            eng.memset(Qbd, 0.0).then_inc(s["qbd_zero"], 1)
            for i in range(2):
                eng.tensor_copy(KT[:, i, :, PAST:PAST + NS], kT[:, :, SP_:T]).then_inc(s["tailk_made"], 1)
            eng.wait_ge(s["out_ps"], NT)
            eng.dma_start(bdn, b_down[0]).then_inc(s["late_in"], 16)
            link(eng.memset(tri, 1.0))
            eng.affine_select(out=tri, in_=tri, compare_op=ALU.is_gt, fill=0.0, base=0,
                              pattern=[[1, 128]], channel_multiplier=-1).then_inc(s["slot_made"], 1)
            eng.wait_ge(s["out_sq"], 1)
            eng.wait_ge(s["x1_made"], 1)
            eng.wait_ge(s["h2_made"], 1)
            eng.wait_ge(s["router_ps"], 1)
            eng.wait_ge(s["h2_ps"], 6)
            eng.dma_start(bgu, b_gate_up[0]).then_inc(s["bgu_in"], 16)
            eng.iota(sioti, pattern=[[1, CAP]], base=0, channel_multiplier=0).then_inc(s["slot_made"], 1)
            eng.iota(eioti, pattern=[[1, E]], base=0, channel_multiplier=0).then_inc(s["slot_made"], 1)
            eng.wait_ge(s["y_made"], 6)
            eng.dma_start(y_prompt[0].rearrange("(t p) n -> p t n", p=128), yrow[:, 0:2, :]).then_inc(s["out_y"], 16)
            eng.dma_start(y_sample.rearrange("b q n -> (b q) n"), yrow[0:NS, 2, :]).then_inc(s["out_y"], 16)
            eng.wait_ge(s["out_y"], 32)
            eng.wait_ge(s["out_kv"], 64)
            eng.wait_ge(s["out_states"], 96)

        def by_sample(v):
            return v[:, :, SP_:T].rearrange("p t (b q) -> p t b q", q=DS)

        def per_sample(v):
            return v[:, :, 1:NR].unsqueeze(3).to_broadcast([128, NT, DB, DS])

        def windows(v, lo, n):
            width = v.shape[2]
            pad = lo + DB * SEG - width
            if pad <= 0:
                return v[:, :, lo:lo + DB * SEG].rearrange("p t (b c) -> p t b c", c=SEG)[:, :, :, 0:n]
            lo2 = lo - pad
            return v[:, :, lo2:lo2 + DB * SEG].rearrange("p t (b c) -> p t b c", c=SEG)[:, :, :, pad:pad + n]

        @block.scalar
        def _(eng):
            link = Chain(eng, s["chain_act"])
            A_ = nc.scalar.activation

            def root(v, n):
                eng.wait_ge(s["ms_made"], n)
                A_(v, v, ACT.Sqrt).then_inc(s["rs_made"], 1)

            eng.wait_ge(s["vec_made"], 1)
            A_(sigc, vec("c", NR * NT), ACT.Sigmoid).then_inc(s["csig_made"], 1)
            for t in range(NT):
                eng.wait_ge(s["xT_made"], t + 1)
                A_(gaT[:, t, :], xT[:, t, :], ACT.Square).then_inc(s["xT_sq"], 1)
            root(rs, 1)
            eng.wait_ge(s["absw_made"], 1)
            A_(t8, s8, ACT.Exp, scale=-1.0).then_inc(s["expw_made"], 1)

            def job(j):
                kind, t = JOBS[j]
                ps = B[4 + j % 4]
                eng.wait_ge(s["job_ps"], j + 1)
                if kind == "a":
                    if t >= 4:
                        eng.wait_ge(s["fold_ps"], t - 3)
                    A_(adarow[:, t % 4, :], ps[:, :], ACT.Copy).then_inc(s["job_ev"], 1)
                elif kind == "v":
                    A_(gbT[:, t, :], ps[:, 0:T], ACT.Copy).then_inc(s["job_ev"], 1)
                elif kind == "k":
                    A_(kT[:, t, :], ps[:, 0:T], ACT.Copy).then_inc(s["job_ev"], 1)
                elif kind == "q":
                    A_(qT[:, t, :], ps[:, 0:T], ACT.Copy, scale=SCALE).then_inc(s["job_ev"], 1)
                elif kind == "x":
                    link(A_(xp[:, t, CW - 1:CW - 1 + SP_], ps[:, 0:SP_], ACT.Copy))
                    A_(windows(xp, S0 + CW - 1, DS)[:, t, :, :], ps[:, SP_:T].rearrange("p (b q) -> p b q", q=DS),
                       ACT.Copy).then_inc(s["job_ev"], 1)
                elif kind == "f":
                    eng.wait_ge(s["small_in"], 64)
                    A_(lfz, ps[0:H, 0:T], ACT.Identity, bias=bfg).then_inc(s["job_ev"], 1)
                elif kind in ("r", "i"):
                    if j == LAST["q"]:
                        eng.wait_ge(s["out_kv"], 64)
                    A_((R if kind == "r" else U)[:, t, :], ps[:, 0:OW], ACT.Sigmoid,
                       bias=vec("rg_b_a" if kind == "r" else "rg_b_x")[:, t:t + 1]).then_inc(s["job_ev"], 1)
                else:
                    if kind == "gb" and t == 0:
                        eng.wait_ge(s["tr_ps"], G_K)
                    A_((gaT if kind == "ga" else gbT)[:, t, :], ps[:, 0:T], ACT.Sigmoid).then_inc(s["job_ev"], 1)

            for j in range(LAST["q"]):
                job(j)
                if j == LAST["f"] + 1:
                    eng.wait_ge(s["absw_made"], 2)
                    A_(Ssb[0:H, 0, 0:T], Ssb[0:H, 0, 0:T], ACT.Exp, scale=-1.0).then_inc(s["expw_made"], 1)
            for j in range(LAST["q"], LAST["i"] + 3):
                job(j)
            eng.wait_ge(s["decay_in"], 1)
            link(A_(A, R, ACT.Exp))
            A_(R, R, ACT.Tanh, scale=-1.0).then_inc(s["decay_out"], 1)
            for j in range(LAST["i"] + 3, LAST["i"] + 7):
                job(j)
            eng.wait_ge(s["den_made"], 1)
            A_(R, R, ACT.Sqrt, scale=2.0).then_inc(s["mult_made"], 1)
            for j in range(LAST["i"] + 7, LAST["gb"]):
                job(j)

            def exps(h):
                eng.wait_ge(s["negmax_made"], h + 1)
                P = Ssb[:, h % 3, :]
                link(A_(P[:, 0:128], P[:, 0:128], ACT.Exp, bias=nm[:, h % 3, 0:1], accum_out=rsum[:, h % 3, 0:1]))
                A_(P[:, 128:384], P[:, 128:384], ACT.Exp, bias=nm[:, h % 3, 1:2],
                   accum_out=rsum[:, h % 3, 1:2]).then_inc(s["exp_done"], 1)

            exps(0)
            exps(1)
            for h in range(H):
                eng.wait_ge(s["PT_ps"], h + 1)
                A_(PTs[:, h % 2, :], B[4 + h % 2][:, 0:384], ACT.Copy).then_inc(s["PT_ev"], 1)
                if h + 2 < H:
                    exps(h + 2)

            def keys(b):
                for g in range(4):
                    n = 4 * b + g
                    eng.wait_ge(s["KT_ps"], n + 1)
                    A_(KT[:, b % 2, 2 * g:2 * g + 2, 0:PAST], B[n % 2][:, :].rearrange("p (t c) -> p t c", t=2),
                       ACT.Copy).then_inc(s["KT_ev"], 1)

            def sexps(b):
                eng.wait_ge(s["snegmax_made"], b + 1)
                A_(Ss[:, b % 2, :], Ss[:, b % 2, :], ACT.Exp, bias=sst[:, b % 2, 0:1],
                   accum_out=sst[:, b % 2, 1:2]).then_inc(s["sexp_done"], 1)

            keys(0)
            keys(1)
            sexps(0)
            for b in range(DB):
                eng.wait_ge(s["sPT_ps"], b + 1)
                link(A_(PT2[:, b % 2, 0:256], B[4 + b % 2][:, 0:256], ACT.Copy))
                A_(PT2[0:NS, b % 2, 256:384], B[4 + b % 2][0:NS, 256:384], ACT.Copy).then_inc(s["sPT_ev"], 1)
                if b + 1 < DB:
                    sexps(b + 1)
                if b + 2 < DB:
                    keys(b + 2)

            for t in range(NT):
                eng.wait_ge(s["out_read"], t + 1)
                A_(kT[:, t, :], qT[:, t, :], ACT.Square).then_inc(s["out_sq"], 1)
            root(rs2, 2)
            for half in range(2):
                eng.wait_ge(s["x1_made"], half + 1)
                if half == 0:
                    eng.wait_ge(s["rs_sq_ps"], 1)
                A_(kT[:, 4 * half:4 * half + 4, :], xT[:, 4 * half:4 * half + 4, :], ACT.Square).then_inc(s["x1_sq"], 1)
            root(rs2, 3)
            eng.wait_ge(s["topmax_made"], 1)
            A_(tope[:, :, 0:TOPK], tope[:, :, 0:TOPK], ACT.Exp).then_inc(s["topexp_made"], 1)

            eng.wait_ge(s["tables_made"], 2)
            link(eng.memzero(Ysb))
            link(eng.memzero(Ccur))
            eng.sem_inc(s["Y_made"], 1)
            eng.sem_inc(s["C_moved"], 1)

            def XT_out(n):
                eng.wait_ge(s["gather_ps"], n)
                for i in range(2):
                    A_(XT[:, 4 * i:4 * i + 4, :], B[4 + i][:, 0:4 * SL].rearrange("p (t s) -> p t s", t=4),
                       ACT.Copy).then_inc(s["XT_made"], 1)

            def C_out(n):
                eng.wait_ge(s["cT_ps"], n)
                A_(Cnext, B[7][0:SL, 0:T], ACT.Copy).then_inc(s["C_made"], 1)

            XT_out(1)
            C_out(1)

            def pair(t, i):
                eng.wait_ge(s["scatter_ps"], NT * t + NT)
                eng.wait_ge(s["C_made"], t + 1)
                A_(Ccur, Cnext, ACT.Copy).then_inc(s["C_moved"], 1)
                eng.wait_ge(s["C_moved"], t + 2)
                C_out(t + 2)
                eng.wait_ge(s["gu_done"], t + 1)
                XT_out(t + 2)
                for j in range(2):
                    eng.wait_ge(s["glu_made"], 2 * t + (j + 1))
                    if j == 0:
                        eng.wait_ge(s["act_made"], 2 * t + 1)
                    A_(sig[:, 512 * j:512 * j + 512], glu[:, 512 * j:512 * j + 512], ACT.Sigmoid, scale=ALPHA)\
                        .then_inc(s["sig_made"], 1)
                for j in range(2):
                    eng.wait_ge(s["aT_ps"], 2 * t + (j + 1))
                    A_(actT[:, 4 * j:4 * j + 4, :], B[j][:, 0:4 * SL].rearrange("p (t s) -> p t s", t=4), ACT.Copy)\
                        .then_inc(s["aT_made"], 1)
                eng.wait_ge(s["dn_done"], t + 2)
                eng.wait_ge(s["C_moved"], t + 2)
                for j in range(2):
                    A_(Ysb[:, 512 * j:512 * j + 512], B[4 + j][:, :], ACT.Copy).then_inc(s["Y_made"], 1)

            done = moe_rounds(eng, pair)
            eng.wait_ge(s["scatter_read"], NT * done + (NT + 1))
            for half in range(2):
                A_(kT[:, 4 * half:4 * half + 4, :], gbT[:, 4 * half:4 * half + 4, :], ACT.Square).then_inc(s["f_sq"], 1)
            root(rs2, 4)

        @block.vector
        def _(eng):
            link = Chain(eng, s["chain_dve"])
            V_ = nc.vector
            TTo, TS, STT = V_.tensor_tensor, V_.tensor_scalar, V_.scalar_tensor_tensor

            def log1p(acc, t, x, w, last):
                link(TS(w, t, 2.0, None, ALU.add))
                link(V_.reciprocal(w, w))
                link(TTo(x, t, w, ALU.mult))
                link(TTo(w, x, x, ALU.mult))
                link(TS(acc, w, 1.0 / 13, None, ALU.mult))
                for d in (11, 9, 7, 5, 3):
                    link(STT(acc, acc, 1.0 / d, w, ALU.add, ALU.mult))
                link(STT(acc, acc, 1.0, x, ALU.add, ALU.mult))

            def rms(dst, ps, n):
                link(TS(dst, ps, 1.0 / D, EPS, ALU.mult, ALU.add))
                V_.reciprocal(dst, dst).then_inc(s["ms_made"], 1)
                eng.wait_ge(s["rs_made"], n)

            def modulate(v, g, shift):
                G_, S_ = Gm[:, g, :, :], ada[:, NT * shift:NT * shift + NT, :]
                for t in range(NT):
                    link.later(TS(v[:, t, 0:SP_], v[:, t, 0:SP_], G_[:, t, 0:1], S_[:, t, 0:1], ALU.mult, ALU.add))
                link(TTo(by_sample(v), by_sample(v), per_sample(G_), ALU.mult))
                link(TTo(by_sample(v), by_sample(v), per_sample(S_), ALU.add))

            def ada_out(lo, hi):
                n = hi - lo
                return TTo(ada[:, lo:hi, :], B[3][:, NR * lo:NR * hi].rearrange("p (m r) -> p m r", r=NR),
                           vecT[:, V["b_ada"] + lo:V["b_ada"] + hi].unsqueeze(2).to_broadcast([128, n, NR]), ALU.add)

            def gain(g, comp, name, plus):
                return STT(Gm[:, g, :, :], ada[:, NT * comp:NT * comp + NT, :], plus,
                           vec(name).unsqueeze(2).to_broadcast([128, NT, NR]), ALU.add, ALU.mult)

            eng.wait_ge(s["ident_made"], 2)
            V_.tensor_copy(qsel.rearrange("q (h c) -> q h c", c=DS), ident[0:DS, 0:DS].unsqueeze(1).to_broadcast([DS, H, DS]))\
                .then_inc(s["qsel_made"], 1)
            eng.wait_ge(s["rows_ps"], 1)
            o = 0
            for i, n in enumerate((96, 120, 64, 96, 96)):
                link(V_.tensor_copy(vecT[:, o:o + n], B[0][:, o:o + n]))
                o += n
            eng.sem_inc(s["vec_made"], 1)
            V_.tensor_copy(smask, B[2][:, 0:2 * NS - DS]).then_inc(s["smask_made"], 1)
            for t in range(NT):
                eng.wait_ge(s["xT_ps"], t + 1)
                V_.tensor_copy(xT[:, t, :], B[4 + t % 4][:, 0:T]).then_inc(s["xT_made"], 1)
            eng.wait_ge(s["csig_made"], 1)
            eng.wait_ge(s["silu_zeroed"], 1)
            TTo(silu_c[:, :, 0:NR], vec("c", NR * NT).rearrange("p (r t) -> p t r", t=NT),
                sigc.rearrange("p (r t) -> p t r", t=NT), ALU.mult).then_inc(s["c_made"], 1)
            groups = ident[:, :].rearrange("p (g h q) -> p g h q", g=4, h=4)
            V_.reduce_sum(fold9, ident[:, :].rearrange("p (g r) -> p r g", g=4)[:, 0:NR, :], AX.X).then_inc(s["c_made"], 1)
            link(V_.reduce_sum(hm4, groups.rearrange("p g h q -> p h g q"), AX.XY))
            STT(s8, vec("rg_lambda"), -1.0, vec("rg_lambda"), ALU.mult, ALU.max).then_inc(s["absw_made"], 1)
            eng.wait_ge(s["sum_ps"], 1)
            rms(rs, B[2][:, 0:T], 1)
            eng.wait_ge(s["xT_made"], NT)
            link(TTo(hT[:, :, :], xT[:, :, :], rs.unsqueeze(1).to_broadcast([128, NT, T]), ALU.mult))
            eng.wait_ge(s["ada_ps"], 1)
            link(ada_out(0, 2 * NT))
            link(gain(0, 1, "g_mix_pre", 1.0))
            modulate(hT, 0, 0)
            eng.sem_inc(s["h_made"], 1)
            eng.wait_ge(s["expw_made"], 1)
            log1p(a8, t8, sp8, s8, 1)
            link(TS(sp8, vec("rg_lambda"), -1.0, 0.0, ALU.mult, ALU.max))
            link(STT(sp8, a8, 2.0, sp8, ALU.mult, ALU.add))
            link(TS(sp8, sp8, -LRU_C, None, ALU.mult))

            def rows_out(g):
                eng.wait_ge(s["tr_ps"], g + 1)
                ps = B[g % 3]
                if g < G_LF:
                    k, half = divmod(g % 6, 2)
                    dst, n = (tok if g < G_K else ktok), TROWS[k]
                    V_.tensor_copy(dst[0:n, k, 512 * half:512 * half + 512], ps[0:n, :]).then_inc(s["tr_ev"], 1)
                elif g < G_CF:
                    for k in range(2):
                        link(V_.tensor_copy(lftok[:, k, :], ps[:, H * k:H * k + H]))
                    V_.tensor_copy(lftok[0:NS, 2, :], ps[0:NS, 2 * H:3 * H]).then_inc(s["tr_ev"], 1)
                elif g < G_ST:
                    b = 2 * (g - G_CF)
                    dst = F[:, SP_:FW].rearrange("h (b c) -> h b c", c=PAST + DS)[:, b:b + 2, 0:PAST]
                    V_.tensor_copy(dst, ps[0:H, :].rearrange("h (b c) -> h b c", b=2)).then_inc(s["tr_ev"], 1)
                else:
                    half = g - G_ST
                    V_.tensor_copy(strow[:, 512 * half:512 * half + 512], ps[0:36, :]).then_inc(s["tr_ev"], 1)

            for g in range(G_LF):
                rows_out(g)
            eng.wait_ge(s["job_ev"], LAST["x"])
            eng.wait_ge(s["xp_edges"], 1)
            for half in range(2):
                n, b0 = DB // 2, half * DB // 2
                st = vecT[:, V["conv"] + 96 * half:V["conv"] + 96 * half + 96].rearrange("p (b j t) -> p t b j", j=CW - 1, t=NT)
                link(V_.tensor_copy(xp[:, :, SP_ + CW - 1:XW].rearrange("p t (b c) -> p t b c", c=SEG)[:, :, b0:b0 + n, 0:CW - 1], st))
            for t in range(NT):
                w = vecT[:, V["conv_w"]:V["conv_w"] + CW * NT].rearrange("p (j t) -> p j t", t=NT)
                link(TS(xc[:, t, :], xp[:, t, 0:OW], w[:, 0, t:t + 1], vec("conv_b")[:, t:t + 1], ALU.mult, ALU.add))
                for j in range(1, CW):
                    ins = STT(xc[:, t, :], xp[:, t, j:j + OW], w[:, j, t:t + 1], xc[:, t, :], ALU.mult, ALU.add)
                    if j < CW - 1:
                        link(ins)
                    else:
                        ins.then_inc(s["conv_made"], 1)
            V_.tensor_copy(hsel.rearrange("k (h c) -> k h c", c=DS), ident[0:H, 0:H].unsqueeze(2).to_broadcast([H, H, DS]))\
                .then_inc(s["hsel_made"], 1)
            w_, t_, x_ = Ssb[0:H, 1, 0:T], Ssb[0:H, 0, 0:T], Ssb[0:H, 2, 0:T]
            eng.wait_ge(s["job_ev"], LAST["f"])
            STT(t_, lfz, -1.0, lfz, ALU.mult, ALU.max).then_inc(s["absw_made"], 1)
            link(V_.tensor_copy(st36[:, :, NR:NR + 3], xp[:, :, SP_:SP_ + 3]))
            link(V_.tensor_copy(st36[:, :, NR + 3:36].rearrange("p t (b j) -> p t b j", j=3),
                                xp[:, :, SP_ + CW - 1:XW].rearrange("p t (b c) -> p t b c", c=SEG)[:, :, :, DS:SEG]))
            eng.wait_ge(s["expw_made"], 2)
            acc_ = PTs[0:H, 0, 0:T]
            log1p(acc_, t_, x_, w_, 1)
            link(TS(lfz, lfz, 0.0, None, ALU.min))
            STT(lfz, acc_, -2.0, lfz, ALU.mult, ALU.add).then_inc(s["lf_made"], 1)
            rows_out(G_LF)
            eng.wait_ge(s["job_ev"], LAST["i"])
            TTo(R, R, sp8.unsqueeze(2).to_broadcast([128, NT, OW]), ALU.mult).then_inc(s["decay_in"], 1)
            link(TTo(U, U, xc, ALU.mult))
            eng.wait_ge(s["decay_out"], 1)
            link(TS(Dn, R, 1.0, None, ALU.add))
            link(V_.reciprocal(Dn, Dn))
            TTo(R, R, Dn, ALU.mult).then_inc(s["den_made"], 1)
            link(V_.memset(A[:, :, 0:1], 0.0))
            link(V_.memset(windows(A, S0 - 1, 1), 0.0))
            eng.wait_ge(s["mult_made"], 1)
            link(V_.memset(R[:, :, 0:1], 1.0))
            link(TTo(U, U, R, ALU.mult))
            link(V_.tensor_copy(windows(U, S0 - 1, 1), vec("h0", 64).rearrange("p (b t) -> p t b", t=NT).unsqueeze(3)))
            link(V_.tensor_tensor_scan(Uf, Af, Uf, 0.0, ALU.mult, ALU.add))
            link(V_.tensor_copy(st36[:, :, 0:1], U[:, :, SP_ - 1:SP_]))
            V_.tensor_copy(st36[:, :, 1:NR].unsqueeze(3), windows(U, S0 + DS - 1, 1)).then_inc(s["st_made"], 1)
            eng.wait_ge(s["job_ev"], LAST["ga"])
            link(TTo(gaT[:, :, 0:SP_], gaT[:, :, 0:SP_], U[:, :, 0:SP_], ALU.mult))
            TTo(by_sample(gaT), by_sample(gaT), windows(U, S0, DS), ALU.mult).then_inc(s["rg_done"], 1)
            eng.wait_ge(s["job_ps"], LAST["gb"])
            link(V_.tensor_copy(F[:, 0:SP_], lfz[:, 0:SP_]))
            link(V_.tensor_copy(F[:, SP_:FW].rearrange("h (b c) -> h b c", c=PAST + DS)[:, :, PAST:PAST + DS],
                                lfz[:, SP_:T].rearrange("h (b q) -> h b q", q=DS)))
            for g in range(G_CF, G_ST):
                rows_out(g)
            eng.wait_ge(s["tr_ev"], G_ST)
            eng.wait_ge(s["consts_made"], 4)
            for lo, n in [(0, SP_)] + [(SP_ + b * (PAST + DS), PAST + DS) for b in range(DB)]:
                link(V_.tensor_tensor_scan(F[:, lo:lo + n], onesf[0:H, 0:n], F[:, lo:lo + n], 0.0, ALU.mult, ALU.add))
            TS(F, F, -1.0, None, ALU.mult).then_inc(s["F_made"], 1)
            rows_out(G_ST)
            rows_out(G_ST + 1)
            eng.wait_ge(s["ada_ps"], 2)
            link(ada_out(2 * NT, 6 * NT))
            link(gain(1, 2, "g_mix_post", 0.0))
            link(gain(2, 4, "g_ffn_pre", 1.0))
            link(gain(3, 5, "g_ffn_post", 0.0))
            eng.wait_ge(s["out_states"], 96)

            def head_max(h):
                eng.wait_ge(s["scores_ps"], h + 1)
                if h >= 3:
                    eng.wait_ge(s["PT_ps"], h - 2)
                P = Ssb[:, h % 3, :]
                TTo(P, B[h % 3][:, 0:384], mask, ALU.add).then_inc(s["scores_read"], 1)
                eng.wait_ge(s["scores_read"], h + 1)
                link(V_.tensor_reduce(nm[:, h % 3, 0:1], P[:, 0:128], AX.X, ALU.max, negate=True))
                V_.tensor_reduce(nm[:, h % 3, 1:2], P[:, 128:384], AX.X, ALU.max, negate=True).then_inc(s["negmax_made"], 1)

            def head_norm(h):
                eng.wait_ge(s["exp_done"], h + 1)
                P, r_ = Ssb[:, h % 3, :], rsum[:, h % 3, :]
                link(V_.reciprocal(r_, r_))
                link(TS(P[:, 0:128], P[:, 0:128], r_[:, 0:1], None, ALU.mult))
                TS(P[:, 128:384], P[:, 128:384], r_[:, 1:2], None, ALU.mult).then_inc(s["probs_made"], 1)

            def head_out(p):
                eng.wait_ge(s["py_ps"], p + 1)
                TTo(gbT[:, p, 0:SP_], gbT[:, p, 0:SP_], B[6 + p % 2][:, 0:SP_], ALU.mult).then_inc(s["py_read"], 1)

            eng.wait_ge(s["job_ev"], LAST["gb"])
            head_max(0)
            head_max(1)
            for h in range(H):
                head_norm(h)
                if h + 2 < H:
                    head_max(h + 2)
                if h % 2 and h >= 3:
                    head_out(h // 2 - 1)
            head_out(H // 2 - 1)

            def queries(b):
                if b == 0:
                    eng.wait_ge(s["qbd_zero"], 1)
                if b >= 2:
                    eng.wait_ge(s["sscores_ps"], b - 1)
                q0 = SP_ + DS * b
                for o in (0, 1):
                    dst = Qbd[64 * o:64 * o + 64, b % 2, :].rearrange("d (t c) -> d t c", c=QB)[:, :, DS * o:DS * o + DS]
                    V_.tensor_copy(dst, qT[64 * o:64 * o + 64, :, q0:q0 + DS]).then_inc(s["qbd_made"], 1)

            def sample_max(b):
                eng.wait_ge(s["sscores_ps"], b + 1)
                P, ps = Ss[:, b % 2, :], B[2 + b % 2]
                if b >= 2:
                    eng.wait_ge(s["sPT_ps"], b - 1)
                V_.tensor_copy(P[:, 0:PAST], ps[:, 0:PAST]).then_inc(s["sscores_read"], 1)
                TTo(P[:, PAST:PAST + NS], ps[:, PAST:PAST + NS], smask[:, NS - DS - DS * b:2 * NS - DS - DS * b],
                    ALU.add).then_inc(s["sscores_read"], 1)
                eng.wait_ge(s["sscores_read"], 2 * b + 2)
                V_.tensor_reduce(sst[:, b % 2, 0:1], P, AX.X, ALU.max, negate=True).then_inc(s["snegmax_made"], 1)

            def sample_norm(b):
                eng.wait_ge(s["sexp_done"], b + 1)
                link(V_.reciprocal(sst[:, b % 2, 2:3], sst[:, b % 2, 1:2]))
                TS(Ss[:, b % 2, :], Ss[:, b % 2, :], sst[:, b % 2, 2:3], None, ALU.mult).then_inc(s["sprobs_made"], 1)

            def own_heads(b):
                eng.wait_ge(s["sv_ps"], b + 1)
                if b >= 2:
                    eng.wait_ge(s["sy_ps"], b - 1)
                TTo(Ym[:, b % 2, :].rearrange("p (h d) -> p h d", h=4), B[6 + b % 2][:, 0:256].rearrange("p (h d) -> p h d", h=4),
                    hm4.unsqueeze(2).to_broadcast([128, 4, HD]), ALU.mult).then_inc(s["sv_made"], 1)

            def sample_out(b):
                eng.wait_ge(s["sy_ps"], b + 1)
                q0 = SP_ + DS * b
                y = B[6 + b % 2][:, 256:320].rearrange("p (h g q) -> p g h q", h=2, g=4)
                dst = gbT[:, :, q0:q0 + DS].rearrange("p (g h) q -> p g h q", h=2)
                TTo(dst, dst, y, ALU.mult).then_inc(s["sy_read"], 1)

            V_.reduce_sum(fold8.rearrange("p (g q) -> p g q", g=4), groups.rearrange("p g h q -> p g q h"), AX.X)\
                .then_inc(s["fold8_made"], 1)
            queries(0)
            queries(1)
            sample_max(0)
            for b in range(DB):
                sample_norm(b)
                if b + 2 < DB:
                    queries(b + 2)
                if b + 1 < DB:
                    sample_max(b + 1)
                own_heads(b)
                if b >= 1:
                    sample_out(b - 1)
            sample_out(DB - 1)
            eng.wait_ge(s["sy_read"], DB)
            eng.wait_ge(s["py_read"], H // 2)
            TTo(gaT[:, :, :], gaT[:, :, :], gbT[:, :, :], ALU.add).then_inc(s["merged"], 1)

            for t in range(NT):
                eng.wait_ge(s["out_ps"], t + 1)
                V_.tensor_copy(qT[:, t, :], B[4 + t % 4][:, 0:T]).then_inc(s["out_read"], 1)
            eng.wait_ge(s["rs_sq_ps"], 1)
            eng.wait_ge(s["out_read"], NT)

            def add_branch(v, rstd, g, sig_):
                for half in range(2):
                    a, z = 4 * half, 4 * half + 4
                    link(TTo(v[:, a:z, :], v[:, a:z, :], rstd.unsqueeze(1).to_broadcast([128, 4, T]), ALU.mult))
                    G_ = Gm[:, g, :, :]
                    for t in range(a, z):
                        link.later(STT(xT[:, t, 0:SP_], v[:, t, 0:SP_], G_[:, t, 0:1], xT[:, t, 0:SP_], ALU.mult, ALU.add))
                    link(TTo(by_sample(v)[:, a:z], by_sample(v)[:, a:z], per_sample(G_)[:, a:z], ALU.mult))
                    TTo(by_sample(xT)[:, a:z], by_sample(xT)[:, a:z], by_sample(v)[:, a:z], ALU.add).then_inc(sig_, 1)

            rms(rs2, B[0][:, 0:T], 2)
            add_branch(qT, rs2, 1, s["x1_made"])
            eng.wait_ge(s["rs_sq_ps"], 2)
            rms(rs2, B[1][:, 0:T], 3)
            eng.wait_ge(s["x1_made"], 2)
            link(TTo(hT[:, :, :], xT[:, :, :], rs2.unsqueeze(1).to_broadcast([128, NT, T]), ALU.mult))
            modulate(hT, 2, 3)
            eng.sem_inc(s["h2_made"], 1)
            eng.wait_ge(s["consts_made"], 4)
            link(V_.tensor_copy(steps, steps_i))
            eng.wait_ge(s["x1_sq"], 2)
            link(V_.memset(lg, 0.0))
            for g in range(6):
                eng.wait_ge(s["h2_ps"], g + 1)
                k, half = divmod(g, 2)
                V_.tensor_copy(tok[0:TROWS[k], k, 512 * half:512 * half + 512], B[2 + g % 2][0:TROWS[k], :]).then_inc(s["h2tok_made"], 1)
            eng.wait_ge(s["router_ps"], 1)
            for k in range(TT):
                link(V_.tensor_copy(lg[0:TROWS[k], k, :], B[4][0:TROWS[k], E * k:E * k + E]))
            for k in range(TT):
                link(V_.max(top[:, k, :], lg[:, k, :]))
                link(V_.max_index(topi[:, k, :], top[:, k, :], lg[:, k, :]))
            link(V_.tensor_copy(topf, topi))
            TTo(tope[:, :, 0:TOPK], top[:, :, 0:TOPK], top[:, :, 0:1].to_broadcast([128, TT, TOPK]), ALU.subtract)\
                .then_inc(s["topmax_made"], 1)
            eng.wait_ge(s["slot_made"], 3)
            link(V_.tensor_copy(slot, sioti))
            link(V_.tensor_copy(exi, eioti))
            eng.wait_ge(s["topexp_made"], 1)
            link(V_.reduce_sum(toks[:, :, 0:1], tope[:, :, 0:TOPK], AX.X))
            link(V_.reciprocal(toks[:, :, 0:1], toks[:, :, 0:1]))
            link(TTo(tope[:, :, 0:TOPK], tope[:, :, 0:TOPK], toks[:, :, 0:1].to_broadcast([128, TT, TOPK]), ALU.mult))
            exb = exi.unsqueeze(1).to_broadcast([128, TT, E])
            for j in range(TOPK):
                link(TTo(hit if j else chosen, exb, topf[:, :, j:j + 1].to_broadcast([128, TT, E]), ALU.is_equal))
                h_ = hit if j else chosen
                if j:
                    link(TTo(chosen, chosen, hit, ALU.add))
                link(TTo(hit if j else wtok, h_, tope[:, :, j:j + 1].to_broadcast([128, TT, E]), ALU.mult))
                if j:
                    link(TTo(wtok, wtok, hit, ALU.add))
            eng.sem_inc(s["chosen_made"], 1)
            eng.wait_ge(s["rank_ps"], 1)
            link(TS(rk0, chosen, 1e6, -1e6, ALU.mult, ALU.add))
            link(TTo(rk0, rk0, B[5][:, 0:TT * E].rearrange("p (t e) -> p t e", t=TT), ALU.add))
            link(V_.reduce_max(cmax, B[5][:, TT * E:TT * E + E], AX.X))
            link(TS(over, steps, cmax, None, ALU.is_lt))
            link(V_.reduce_sum(rounds_f, over, AX.X))
            V_.tensor_copy(rounds_i, rounds_f).then_inc(s["rounds_made"], 1)
            for r in range(ROUNDS + 1):
                link(TS(rank[:, :, E * r:E * r + E], rk0, float(-CAP * r), None, ALU.add))
                link(V_.tensor_copy(gate[:, :, E * r:E * r + E], wtok))
            eng.wait_ge(s["wt_ps"], 1)
            V_.tensor_copy(WT, B[6][0:E, 0:T]).then_inc(s["wt_made"], 1)
            for t in range(NT):
                eng.wait_ge(s["fT_ps"], t + 1)
                V_.tensor_copy(gbT[:, t, :], B[3 + t % 2][:, 0:T]).then_inc(s["fT_made"], 1)
            eng.wait_ge(s["fT_made"], NT)
            eng.sem_inc(s["act_made"], 2)
            eng.sem_inc(s["lin_made"], 2)
            eng.sem_inc(s["scatter_read"], 1)
            eng.sem_inc(s["tables_made"], 2)

            def select(n, col):
                if not (isinstance(n, int) and n == 0):
                    eng.wait_ge(s["cT_ps"], n)
                shape = [128, TT, 2, CAP]
                rk, gt = (v[:, :, ds(col, 2)].unsqueeze(3).to_broadcast(shape) for v in (rank, gate))
                P4, W4 = (v.rearrange("p t (e s) -> p t e s", e=2) for v in (sel, selw))
                V_.tensor_tensor(P4, slot.unsqueeze(1).unsqueeze(1).to_broadcast(shape), rk, ALU.is_equal).then_inc(s["sel_made"], 1)
                eng.wait_ge(s["sel_made"], 2 * n + 1)
                V_.tensor_tensor(W4, P4, gt, ALU.mult).then_inc(s["sel_made"], 1)

            select(0, 0)
            select(1, 2)
            def experts(i):
                V_.tensor_copy(esel.rearrange("e (two c) -> e two c", two=2),
                               ident[0:E, ds(2 * i, 2)].unsqueeze(2).to_broadcast([E, 2, CAP])).then_inc(s["esel_made"], 1)

            def pair(t, i):
                experts(i)
                for m in range(NT):
                    combined(t, m)
                eng.wait_ge(s["gu_done"], t + 1)
                half = [slice(0, 512), slice(512, 1024)]
                for j, c in enumerate(half):
                    TS(glu[:, c], B[j][:, :], LIMIT, None, ALU.min).then_inc(s["glu_made"], 1)
                for j, c in enumerate(half):
                    TS(lin[:, c], B[2 + j][:, :], LIMIT, -LIMIT, ALU.min, ALU.max).then_inc(s["lin_made"], 1)
                for j, c in enumerate(half):
                    eng.wait_ge(s["glu_made"], 2 * t + (j + 1))
                    eng.wait_ge(s["lin_made"], 4 * t + (j + 3))
                    STT(lin[:, c], lin[:, c], 1.0, glu[:, c], ALU.add, ALU.mult).then_inc(s["lin_made"], 1)
                for j, c in enumerate(half):
                    eng.wait_ge(s["lin_made"], 4 * t + (j + 5))
                    eng.wait_ge(s["sig_made"], 2 * t + (j + 1))
                    TTo(glu[:, c], lin[:, c], sig[:, c], ALU.mult).then_inc(s["act_made"], 1)
                select(t + 2, 2 * t + 4)
                eng.wait_ge(s["scatter_read"], NT * t + (NT + 1))
                eng.wait_ge(s["aT_ps"], 2 * t + 2)

            def combined(t, m):
                eng.wait_ge(s["scatter_ps"], NT * t + m + 1)
                TTo(gbT[:, m, :], gbT[:, m, :], B[6 + m % 2][:, 0:T], ALU.add).then_inc(s["scatter_read"], 1)

            done = moe_rounds(eng, pair)
            for m in range(NT):
                combined(done, m)
            eng.wait_ge(s["f_sum"], 1)
            eng.wait_ge(s["scatter_read"], NT * done + (NT + 1))
            rms(rs2, B[0][:, 0:T], 4)
            add_branch(gbT, rs2, 3, s["y_ready"])
            for g in range(6):
                eng.wait_ge(s["y_ps"], g + 1)
                k, half = divmod(g, 2)
                V_.tensor_copy(yrow[0:TROWS[k], k, 512 * half:512 * half + 512], B[1 + g % 2][0:TROWS[k], :]).then_inc(s["y_made"], 1)

        @block.tensor
        def _(eng):
            mm = nc.tensor.matmul

            def tr(out, in_, rows):
                return nc.tensor.transpose(out, in_, ident[0:rows, 0:rows])

            used = [0]

            def chunk():
                c = used[0]
                used[0] += 1
                eng.wait_ge(chunk_in[c % 3], 16 * (c // 3 + 1))
                return wstage[c % 3]

            eng.wait_ge(s["ident_made"], 2)
            eng.wait_ge(s["rows_in"], 16 * 15)
            eng.wait_ge(s["smask8_made"], 1)
            o = 0
            for i, n in enumerate((96, 120, 64, 96, 96)):
                tr(B[0][:, o:o + n], vrows[0:n, i, :], n)
                o += n
            eng.wait_ge(s["qsel_made"], 1)
            mm(B[2][:, 0:2 * NS - DS], qsel, smask8,
               start=True, stop=True).then_inc(s["rows_ps"], 1)
            eng.wait_ge(s["x_in"], 32)
            for t in range(NT):
                if t >= 4:
                    eng.wait_ge(s["xT_made"], t - 3)
                for k in range(TT):
                    last = tr(B[4 + t % 4][:, 128 * k:128 * k + TROWS[k]], tok[0:TROWS[k], k, 128 * t:128 * t + 128], TROWS[k])
                last.then_inc(s["xT_ps"], 1)

            def sums(bank, sq, sq_sem, steps_):
                for t in range(NT):
                    if t in steps_:
                        eng.wait_ge(sq_sem, steps_[t])
                    last = mm(bank[:, 0:T], ones[:, :], sq[:, t, :], start=(t == 0), stop=(t == NT - 1))
                return last

            eng.wait_ge(s["smask_made"], 1)
            sums(B[2], gaT, s["xT_sq"], {t: t + 1 for t in range(NT)}).then_inc(s["sum_ps"], 1)

            def transposes(g):
                if g >= 3:
                    eng.wait_ge(s["tr_ev"], g - 2)
                ps = B[g % 3]
                if g < G_LF:
                    k, half = divmod(g % 6, 2)
                    src = gbT if g < G_K else kT
                    for i in range(4):
                        last = tr(ps[0:TROWS[k], 128 * i:128 * i + 128], src[:, 4 * half + i, 128 * k:128 * k + TROWS[k]], 128)
                elif g < G_CF:
                    eng.wait_ge(s["lf_made"], 1)
                    for k in range(TT):
                        last = tr(ps[0:TROWS[k], H * k:H * k + H], lfz[:, 128 * k:128 * k + TROWS[k]], H)
                elif g < G_ST:
                    for i in range(4):
                        last = tr(ps[0:H, 128 * i:128 * i + 128], lfc[:, 4 * (g - G_CF) + i, :], 128)
                else:
                    for i in range(4):
                        last = tr(ps[0:36, 128 * i:128 * i + 128], st36[:, 4 * (g - G_ST) + i, :], 128)
                last.then_inc(s["tr_ps"], 1)

            def fold(c):
                eng.wait_ge(s["job_ev"], JOBS.index(("a", c)) + 1)
                for m in range(4):
                    last = mm(B[3][:, NR * (4 * c + m):NR * (4 * c + m + 1)], adarow[:, c % 4, 128 * m:128 * m + 128],
                              fold9, start=True, stop=True)
                last.then_inc(s["fold_ps"], 1)

            eng.wait_ge(s["c_made"], 2)
            eng.wait_ge(s["xT_made"], NT)
            w = None
            for j, (kind, t) in enumerate(JOBS):
                if j == 4:
                    for c in range(4):
                        fold(c)
                    eng.wait_ge(s["fold_ps"], 4)
                    eng.sem_inc(s["ada_ps"], 1)
                    eng.wait_ge(s["h_made"], 1)
                if j >= 4:
                    eng.wait_ge(s["job_ev"], j - 3)
                ps = B[4 + j % 4]
                if kind == "a":
                    w = chunk()
                    for k in range(NT):
                        g = k % 4
                        last = mm(ps[32 * g:32 * g + 32, :], silu_c[:, k, :], w[:, k, :], start=(k < 4), stop=(k >= 4))
                    last.then_inc(s["job_ps"], 1)
                elif kind == "f":
                    eng.wait_ge(s["small_in"], 64)
                    for k in range(NT):
                        last = mm(ps[0:H, 0:T], wf[:, k, :], hT[:, k, :], start=(k == 0), stop=(k == NT - 1))
                    last.then_inc(s["job_ps"], 1)
                elif kind in ("r", "i"):
                    if t == 0:
                        eng.wait_ge(s["rgw_in"], 64)
                    if kind == "r":
                        eng.wait_ge(s["conv_made"], t + 1)
                    mm(ps[:, 0:OW], wax[:, "ri".index(kind), t, :], xc[:, t, :], start=True, stop=True).then_inc(s["job_ps"], 1)
                else:
                    if t % 4 == 0:
                        w = chunk()
                    for k in range(NT):
                        last = mm(ps[:, 0:T], w[:, k, 128 * (t % 4):128 * (t % 4) + 128], hT[:, k, :],
                                  start=(k == 0), stop=(k == NT - 1))
                    last.then_inc(s["job_ps"], 1)
                if kind == "a" or kind in ZCOL and t % 4 == 3:
                    eng.wait_ge(s["job_ps"], j + 1)
                    eng.sem_inc(s["chunk_free"], 1)
                if j > 4 and JOBS[j - 1][0] == "a":
                    fold(JOBS[j - 1][1])
                    if JOBS[j - 1] == ("a", 11):
                        eng.wait_ge(s["fold_ps"], 12)
                        eng.sem_inc(s["ada_ps"], 1)
                if j == LAST["v"] + 5:
                    eng.wait_ge(s["job_ev"], LAST["v"])
                    for g in range(G_V, G_K):
                        transposes(g)
                if j == LAST["k"] + 5:
                    for g in range(G_K, G_LF):
                        transposes(g)
                if kind == "r" and t == NT - 1:
                    transposes(G_LF)
            eng.wait_ge(s["cachef_in"], 16 * DB * NPG)
            for g in range(G_CF, G_ST):
                transposes(g)
            eng.wait_ge(s["st_made"], 1)
            for g in (G_ST, G_ST + 1):
                transposes(g)

            eng.wait_ge(s["F_made"], 1)
            eng.wait_ge(s["hsel_made"], 1)
            eng.wait_ge(s["tr_ev"], G_ST + 2)
            eng.wait_ge(s["job_ev"], LAST["gb"])

            def scores(h):
                p, o = h // 2, 64 * (h % 2)
                if h >= 3:
                    eng.wait_ge(s["scores_read"], h - 2)
                row = ident[0:H, h:h + 1].to_broadcast([H, 128])
                for c, q, n in ((0, 0, 128), (128, 128, 256)):
                    mm(B[h % 3][:, c:c + n], qT[o:o + 64, p, q:q + 128], kT[o:o + 64, p, 0:n], start=True, stop=False)
                    last = mm(B[h % 3][:, c:c + n], row, F[:, 0:n], start=False, stop=True)
                last.then_inc(s["scores_ps"], 1)

            def weights(h):
                eng.wait_ge(s["probs_made"], h + 1)
                if h >= 2:
                    eng.wait_ge(s["PT_ev"], h - 1)
                for i in range(3):
                    last = tr(B[4 + h % 2][:, 128 * i:128 * i + 128], Ssb[:, h % 3, 128 * i:128 * i + 128], 128)
                last.then_inc(s["PT_ps"], 1)

            def values(h):
                p, o = h // 2, 64 * (h % 2)
                eng.wait_ge(s["PT_ev"], h + 1)
                if h % 2 == 0 and p >= 2:
                    eng.wait_ge(s["py_read"], p - 1)
                out = B[6 + p % 2][o:o + 64, :]
                mm(out[:, 0:256], tok[:, 0, HD * h:HD * h + HD], PTs[:, h % 2, 0:256], start=True, stop=False)
                last = mm(out[:, 128:256], tok[:, 1, HD * h:HD * h + HD], PTs[:, h % 2, 256:384], start=False, stop=True)
                if h % 2:
                    last.then_inc(s["py_ps"], 1)

            scores(0)
            scores(1)
            for h in range(H):
                if h + 2 < H:
                    scores(h + 2)
                if h >= 1:
                    values(h - 1)
                weights(h)
            values(H - 1)

            def keysT(b):
                eng.wait_ge(k_in[b % 2], 16 * NPG * (b // 2 + 1))
                for g in range(4):
                    n = 4 * b + g
                    if n >= 2:
                        eng.wait_ge(s["KT_ev"], n - 1)
                    for i in range(2):
                        for j in range(NPG):
                            last = tr(B[n % 2][:, PAST * i + 128 * j:PAST * i + 128 * j + 128],
                                      kv[:, b % 2, j, 128 * (2 * g + i):128 * (2 * g + i) + 128], 128)
                    last.then_inc(s["KT_ps"], 1)

            def sscores(b):
                eng.wait_ge(s["KT_ev"], 4 * b + 4)
                eng.wait_ge(s["qbd_made"], 2 * b + 2)
                if b >= 2:
                    eng.wait_ge(s["sscores_read"], 2 * (b - 1))
                ps = B[2 + b % 2]
                f0 = SP_ + b * (PAST + DS)
                for odd in range(2):
                    for g in range(4):
                        p = 2 * g + odd
                        q0 = QB * p - 2 * DS * odd
                        mm(ps[32 * g:32 * g + 32, 0:PAST + NS], Qbd[:, b % 2, q0:q0 + 32], KT[:, b % 2, p, :],
                           start=(odd == 0), stop=False)
                mm(ps[:, 0:PAST], hsel, F[:, f0:f0 + PAST], start=False, stop=False)
                mm(ps[:, PAST + DS * b:PAST + DS * b + DS], hsel, F[:, f0 + PAST:f0 + PAST + DS], start=False, stop=True)\
                    .then_inc(s["sscores_ps"], 1)

            def sweights(b):
                eng.wait_ge(s["sprobs_made"], b + 1)
                if b >= 2:
                    eng.wait_ge(s["sPT_ev"], b - 1)
                ps = B[4 + b % 2]
                tr(ps[:, 0:128], Ss[:, b % 2, 0:128], 128)
                tr(ps[:, 128:256], Ss[:, b % 2, 128:256], 128)
                tr(ps[0:NS, 256:384], Ss[:, b % 2, PAST:PAST + NS], 128).then_inc(s["sPT_ps"], 1)

            def svalues(b):
                eng.wait_ge(s["sPT_ev"], b + 1)
                eng.wait_ge(v_in[b % 2], 16 * NPG * (b // 2 + 1))
                if b >= 2:
                    eng.wait_ge(s["sy_read"], b - 1)
                for j in range(NPG + 1):
                    for g in range(4):
                        c = slice(256 * g, 256 * g + 256)
                        n = 128 if j < NPG else NS
                        vals = kv[:, b % 2, NPG + j, c] if j < NPG else tok[0:NS, 2, c]
                        last = mm(B[6 + b % 2][32 * g:32 * g + 32, 0:256], PT2[0:n, b % 2, 128 * j + 32 * g:128 * j + 32 * g + 32],
                                  vals, start=(j == 0), stop=(j == NPG))
                last.then_inc(s["sv_ps"], 1)

            def sfold(b):
                eng.wait_ge(s["sv_made"], b + 1)
                for h in range(2):
                    last = mm(B[6 + b % 2][:, 256 + 32 * h:256 + 32 * h + 32], Ym[:, b % 2, 128 * h:128 * h + 128], fold8,
                              start=True, stop=True)
                last.then_inc(s["sy_ps"], 1)

            eng.wait_ge(s["py_read"], H // 2)
            keysT(0)
            eng.wait_ge(s["tailk_made"], 2)
            eng.wait_ge(s["fold8_made"], 1)
            sscores(0)
            keysT(1)
            for b in range(DB):
                if b + 1 < DB:
                    sscores(b + 1)
                sweights(b)
                svalues(b)
                if b + 2 < DB:
                    keysT(b + 2)
                sfold(b)
            eng.wait_ge(s["sy_ps"], DB)
            eng.sem_inc(s["dn_free"], 4)

            eng.wait_ge(s["merged"], 1)
            for t in range(NT):
                if t % 4 == 0:
                    w = chunk()
                if t >= 4:
                    eng.wait_ge(s["out_read"], t - 3)
                for k in range(NT):
                    last = mm(B[4 + t % 4][:, 0:T], w[:, k, 128 * (t % 4):128 * (t % 4) + 128], gaT[:, k, :],
                              start=(k == 0), stop=(k == NT - 1))
                last.then_inc(s["out_ps"], 1)
            eng.wait_ge(s["out_ps"], NT)
            eng.sem_inc(s["gu_free"], 4)
            sums(B[0], kT, s["out_sq"], {t: t + 1 for t in range(NT)}).then_inc(s["rs_sq_ps"], 1)
            sums(B[1], kT, s["x1_sq"], {0: 1, 4: 2}).then_inc(s["rs_sq_ps"], 1)
            eng.wait_ge(s["h2_made"], 1)
            for g in range(6):
                k, half = divmod(g, 2)
                if g >= 2:
                    eng.wait_ge(s["h2tok_made"], g - 1)
                for i in range(4):
                    last = tr(B[2 + g % 2][0:TROWS[k], 128 * i:128 * i + 128], hT[:, 4 * half + i, 128 * k:128 * k + TROWS[k]], 128)
                last.then_inc(s["h2_ps"], 1)
            for k in range(TT):
                n = TROWS[k]
                ps = B[4][0:n, E * k:E * k + E]
                for t in range(NT):
                    mm(ps, hT[:, t, 128 * k:128 * k + n], wr[:, t, :], start=(t == 0), stop=False)
                last = mm(ps, ones[0:1, 0:n], brow, start=False, stop=True)
            last.then_inc(s["router_ps"], 1)
            eng.wait_ge(s["late_in"], 16)
            eng.wait_ge(s["chosen_made"], 1)
            eng.wait_ge(s["slot_made"], 1)
            for k in range(TT + 1):
                ps = B[5][:, E * k:E * k + E]
                for j in range(min(k, TT - 1) + 1):
                    n = TROWS[j]
                    last = mm(ps, (tri if j == k else ones)[0:n, :], chosen[0:n, j, :], start=(j == 0), stop=(j == min(k, TT - 1)))
            last.then_inc(s["rank_ps"], 1)
            for k in range(TT):
                last = tr(B[6][0:E, 128 * k:128 * k + TROWS[k]], wtok[0:TROWS[k], k, :], TROWS[k])
            last.then_inc(s["wt_ps"], 1)
            eng.wait_ge(s["wt_made"], 1)
            for t in range(NT):
                if t >= 2:
                    eng.wait_ge(s["fT_made"], t - 1)
                mm(B[3 + t % 2][:, 0:T], bdn[:, 128 * t:128 * t + 128], WT, start=True, stop=True).then_inc(s["fT_ps"], 1)
            eng.wait_ge(s["tables_made"], 2)

            eng.wait_ge(s["bgu_in"], 16)

            def gather(n):
                eng.wait_ge(s["sel_made"], 2 * n)
                for m in range(NT):
                    out = B[4 + m // 4][:, SL * (m % 4):SL * (m % 4) + SL]
                    for k in range(TT):
                        r = TROWS[k]
                        last = mm(out, tok[0:r, k, 128 * m:128 * m + 128], sel[0:r, k, :], start=(k == 0), stop=(k == TT - 1))
                last.then_inc(s["gather_ps"], 1)

            def combiner(n):
                for k in range(TT):
                    r = TROWS[k]
                    last = tr(B[7][0:SL, 128 * k:128 * k + r], selw[0:r, k, :], r)
                last.then_inc(s["cT_ps"], 1)

            def combine(n, tiles):
                eng.wait_ge(s["C_moved"], n + 1)
                eng.wait_ge(s["Y_made"], 2 * n + 1)
                for m in tiles:
                    eng.wait_ge(s["scatter_read"], NT * n + (m if m >= 2 else 1))
                    mm(B[6 + m % 2][:, 0:T], Ysb[:, 128 * m:128 * m + 128], Ccur, start=True, stop=True)\
                        .then_inc(s["scatter_ps"], 1)

            def both(bank, lhsT, rhs, start, stop):
                for x in range(2):
                    last = mm(bank[CAP * x:CAP * x + CAP, :], lhsT[:, CAP * x:CAP * x + CAP], rhs(x), start=start, stop=stop)
                return last

            eng.sem_inc(s["dn_done"], 1)
            gather(1)
            combiner(1)

            def pair(t, i):
                eng.wait_ge(s["XT_made"], 2 * t + 2)
                eng.wait_ge(s["lin_made"], 4 * t + 2)
                eng.wait_ge(s["C_made"], t + 1)
                for k in range(NT):
                    eng.wait_ge(gu_in[k % 4], 32 * t + (16 if k < 4 else 32))
                    for j in range(4):
                        last = both(B[j], XT[:, k, :], lambda x: wgu[:, k % 4, x, 512 * j:512 * j + 512], k == 0, k == NT - 1)
                    last.then_inc(s["gu_free"], 1)
                    if k < 4:
                        combine(t, (2 * k, 2 * k + 1))
                    if k == 4:
                        gather(t + 2)
                    if k == 5:
                        eng.wait_ge(s["scatter_read"], NT * t + (NT + 1))
                        combiner(t + 2)
                    if k == 6:
                        eng.wait_ge(s["esel_made"], t + 1)
                        for j in range(4):
                            both(B[j], esel, lambda x: bgu[:, 512 * j:512 * j + 512], False, False)
                eng.wait_ge(s["gu_free"], NT * t + (NT + 4))
                eng.sem_inc(s["gu_done"], 1)
                for j in range(2):
                    eng.wait_ge(s["act_made"], 2 * t + (j + 3))
                    for m in range(4):
                        last = tr(B[j][:, SL * m:SL * m + SL], glu[:, 512 * j + 128 * m:512 * j + 128 * m + 128], 128)
                    last.then_inc(s["aT_ps"], 1)
                eng.wait_ge(s["XT_made"], 2 * t + 4)
                for k in range(NT):
                    if k % 4 == 0:
                        eng.wait_ge(s["aT_made"], 2 * t + (k // 4 + 1))
                    eng.wait_ge(dn_in[k % 4], 32 * t + (16 if k < 4 else 32))
                    for j in range(2):
                        last = both(B[4 + j], actT[:, k, :], lambda x: wdn[:, k % 4, x, 512 * j:512 * j + 512], k == 0, k == NT - 1)
                    if k < NT - 1:
                        last.then_inc(s["dn_free"], 1)
                    else:
                        last.then_inc(s["dn_done"], 1)
                        eng.wait_ge(s["dn_done"], t + 2)
                        eng.sem_inc(s["dn_free"], 1)

            done = moe_rounds(eng, pair)
            combine(done, range(NT))
            sums(B[0], kT, s["f_sq"], {0: 1, 4: 2}).then_inc(s["f_sum"], 1)
            for g in range(6):
                k, half = divmod(g, 2)
                eng.wait_ge(s["y_ready"], half + 1 if g < 2 else 2)
                if g >= 2:
                    eng.wait_ge(s["y_made"], g - 1)
                for i in range(4):
                    last = tr(B[1 + g % 2][0:TROWS[k], 128 * i:128 * i + 128], xT[:, 4 * half + i, 128 * k:128 * k + TROWS[k]], 128)
                last.then_inc(s["y_ps"], 1)


_INS = ['x_prompt', 'x_sample', 'cache_k', 'cache_v', 'cache_logf', 'state_conv', 'state_h', 'page_table',
        'c_prompt', 'c_sample', 'w_ada', 'b_ada', 'g_mix_pre', 'g_mix_post', 'w_in', 'b_forget',
        'conv_w', 'conv_b', 'rg_w_a', 'rg_b_a', 'rg_w_x', 'rg_b_x', 'rg_lambda', 'w_out',
        'g_ffn_pre', 'g_ffn_post', 'w_router', 'b_router', 'w_gate_up', 'b_gate_up', 'w_down', 'b_down']


def kernel(**inputs):
    import numpy as _np
    import concourse.bacc as _bacc
    from concourse import mybir as _mybir
    from concourse.bass_utils import run_bass_kernel_spmd as _run

    nc = _bacc.Bacc("TRN2", target_bir_lowering=False, num_devices=1)
    arrays, args = {}, []
    for name in _INS:
        a = _np.ascontiguousarray(inputs[name])
        arrays[f"in_{name}_dram"] = a
        args.append(nc.dram_tensor(f"in_{name}_dram", a.shape, _mybir.dt.from_np(a.dtype), kind="ExternalInput").ap())
    xs, xd = inputs['x_prompt'].shape, inputs['x_sample'].shape
    heads, hd = inputs['cache_k'].shape[3:]
    conv = inputs['state_conv'].shape
    outs = [xs, xd]
    for n, m in ((xs[0], xs[1]), (xd[0], xd[1])):
        outs += [(1, n, m, heads, hd), (1, n, m, heads, hd), (1, n, m, heads), (1, n, conv[2], conv[3]), (1, n, conv[3])]
    for i, shape in enumerate(outs):
        args.append(nc.dram_tensor(f"out_{i}_dram", shape, _mybir.dt.float32, kind="ExternalOutput").ap())
    hybrid_layer(nc, *args)
    r = _run(nc, [arrays], core_ids=[0])
    return tuple(r.results[0][f"out_{i}_dram"] for i in range(len(outs)))
```
